# Optimizing a Trainium2 kernel written in Bass

```python
import math
import jax
import jax.numpy as jnp
from jax import lax
import numpy as np

D_MODEL = 1024
BATCH = 1
SEQ = 256
DEPTH = 2

GRID_W = 64
CTX_LEN = 256
HEAD_DIM = 64
ROPE_THETA = 10000.0
NORM_EPS = 1e-6
Q_BLOCK = 128
ATTN_SCALE = HEAD_DIM ** -0.5

GDN_HEADS = 4
GDN_DK = 64
GDN_DV = 64
GDN_CONV = 5
GDN_CHUNK = 64
GDN_CONV_CH = 2 * GDN_HEADS * GDN_DK + GDN_HEADS * GDN_DV

MLA_HEADS = 4
MLA_Q_RANK = 256
MLA_KV_RANK = 128
MLA_NOPE = 64
MLA_ROPE = 32
MLA_V = 64
MLA_SCALE = (MLA_NOPE + MLA_ROPE) ** -0.5

SWA_HEADS = 4
SWA_KV_HEADS = 2
WINDOW = 128

GQA_HEADS = 4
GQA_KV_HEADS = 2

D_MIX = GDN_HEADS * GDN_DV + MLA_HEADS * MLA_V + SWA_HEADS * HEAD_DIM + GQA_HEADS * HEAD_DIM

IN_SPLITS = (
    GDN_HEADS * GDN_DK, GDN_HEADS * GDN_DK, GDN_HEADS * GDN_DV, GDN_HEADS * GDN_DV,
    2 * GDN_HEADS, 2 * GDN_HEADS,
    MLA_Q_RANK, MLA_KV_RANK, MLA_ROPE,
    SWA_HEADS * HEAD_DIM, SWA_KV_HEADS * HEAD_DIM, SWA_KV_HEADS * HEAD_DIM,
    GQA_HEADS * HEAD_DIM, GQA_KV_HEADS * HEAD_DIM, GQA_KV_HEADS * HEAD_DIM,
)
D_IN = sum(IN_SPLITS)

N_EXPERTS = 64
TOP_K = 6
D_EXPERT = 384
ROUTED_SCALE = 2.5
MOE_BLOCK = 128

kernel_name = 'hybrid_dit_prefix_block'

def rms_norm(x, g):
    xf = x.astype(jnp.float32)
    y = xf * lax.rsqrt(jnp.mean(xf * xf, axis=-1, keepdims=True) + NORM_EPS)
    return (y * g.astype(jnp.float32)).astype(x.dtype)

def l2_normalize(x):
    return x * lax.rsqrt(jnp.sum(x * x, axis=-1, keepdims=True) + NORM_EPS)

def modulate(h, shift, scale):
    return h * (1 + scale) + shift

def swiglu(x, w_gu, w_down):
    g, u = jnp.split(x @ w_gu, 2, axis=-1)
    return (jax.nn.silu(g) * u) @ w_down

def split_columns(p):
    idx = [int(i) for i in np.cumsum(IN_SPLITS)[:-1]]
    return jnp.split(p, idx, axis=-1)

def axial_rope_tables(n_rows, rot_dim):
    rows = jnp.repeat(jnp.arange(n_rows), GRID_W).astype(jnp.float32)
    cols = jnp.tile(jnp.arange(GRID_W), n_rows).astype(jnp.float32)
    axis_dim = rot_dim // 2
    inv_freq = ROPE_THETA ** (-jnp.arange(0, axis_dim, 2, dtype=jnp.float32) / axis_dim)
    ang_r = rows[:, None] * inv_freq
    ang_c = cols[:, None] * inv_freq
    ang = jnp.concatenate([ang_r, ang_r, ang_c, ang_c], axis=-1)
    return jnp.cos(ang), jnp.sin(ang)

def rotate_half(x):
    x1, x2 = jnp.split(x, 2, axis=-1)
    return jnp.concatenate([-x2, x1], axis=-1)

def apply_axial_rope(x, rope):
    cos, sin = rope
    xr, xc = jnp.split(x, 2, axis=-1)
    rot = jnp.concatenate([rotate_half(xr), rotate_half(xc)], axis=-1)
    out = x.astype(jnp.float32) * cos[None, :, None, :] + rot.astype(jnp.float32) * sin[None, :, None, :]
    return out.astype(x.dtype)

def depthwise_conv_centred(x, w):
    k = w.shape[0]
    return lax.conv_general_dilated(
        x, w[:, None, :].astype(x.dtype), window_strides=(1,), padding=[((k - 1) // 2, k // 2)],
        dimension_numbers=('NWC', 'WIO', 'NWC'), feature_group_count=x.shape[-1])

def gated_delta_chunked(q, k, v, log_a, beta, s0):
    bsz, nh, t_len, dk = q.shape
    dv = v.shape[-1]
    c = GDN_CHUNK
    n = t_len // c
    q = q.reshape(bsz, nh, n, c, dk)
    k = k.reshape(bsz, nh, n, c, dk)
    v = v.reshape(bsz, nh, n, c, dv)
    beta = beta.reshape(bsz, nh, n, c)
    g = jnp.cumsum(log_a.reshape(bsz, nh, n, c), axis=-1)
    incl = jnp.tril(jnp.ones((c, c), bool))
    strict = jnp.tril(jnp.ones((c, c), bool), -1)
    decay_ij = jnp.exp(jnp.where(incl, g[..., :, None] - g[..., None, :], -jnp.inf))
    kb = k * beta[..., None]
    a_mat = jnp.where(strict, jnp.einsum('bhncd,bhnsd->bhncs', kb, k) * decay_ij, 0.0)
    eye = jnp.eye(c, dtype=jnp.float32)
    t_inv = lax.linalg.triangular_solve(eye + a_mat, jnp.broadcast_to(eye, a_mat.shape),
                                        left_side=True, lower=True, unit_diagonal=True)
    u = t_inv @ (v * beta[..., None])
    w = t_inv @ (kb * jnp.exp(g)[..., None])
    qk = jnp.einsum('bhncd,bhnsd->bhncs', q, k) * decay_ij

    def step(s, xs):
        q_i, k_i, u_i, w_i, g_i, qk_i = xs
        v_new = u_i - jnp.einsum('bhcd,bhde->bhce', w_i, s)
        o_i = (jnp.einsum('bhcd,bhde->bhce', q_i * jnp.exp(g_i)[..., None], s)
               + jnp.einsum('bhcs,bhse->bhce', qk_i, v_new))
        g_last = g_i[..., -1:]
        s = (s * jnp.exp(g_last)[..., None]
             + jnp.einsum('bhcd,bhce->bhde', k_i * jnp.exp(g_last - g_i)[..., None], v_new))
        return s, o_i

    xs = tuple(jnp.moveaxis(a, 2, 0) for a in (q, k, u, w, g, qk))
    s_fin, o = lax.scan(step, s0, xs)
    return jnp.moveaxis(o, 0, 2).reshape(bsz, nh, t_len, dv), s_fin

def gdn_prepare(q, k, v, a, b, conv_w, a_log, dt_bias):
    bsz, t_len, _ = q.shape
    qkv = jax.nn.silu(depthwise_conv_centred(jnp.concatenate([q, k, v], axis=-1), conv_w)).astype(jnp.float32)
    q, k, v = jnp.split(qkv, [GDN_HEADS * GDN_DK, 2 * GDN_HEADS * GDN_DK], axis=-1)
    q = l2_normalize(q.reshape(bsz, t_len, GDN_HEADS, GDN_DK)) * GDN_DK ** -0.5
    k = l2_normalize(k.reshape(bsz, t_len, GDN_HEADS, GDN_DK))
    v = v.reshape(bsz, t_len, GDN_HEADS, GDN_DV)
    a = a.astype(jnp.float32).reshape(bsz, t_len, 2, GDN_HEADS)
    b = b.astype(jnp.float32).reshape(bsz, t_len, 2, GDN_HEADS)
    log_a = -jnp.exp(a_log.astype(jnp.float32)) * jax.nn.softplus(a + dt_bias.astype(jnp.float32))
    beta = jax.nn.sigmoid(b)
    to_bhtd = lambda t: t.transpose(0, 2, 1, 3)
    return (to_bhtd(q), to_bhtd(k), to_bhtd(v),
            log_a.transpose(2, 0, 3, 1), beta.transpose(2, 0, 3, 1))

def gdn_bidirectional(ctx_in, lat_in):
    qc, kc, vc, lac, bc = ctx_in
    ql, kl, vl, lal, bl = lat_in
    bsz, nh, _, dk = qc.shape
    s0 = jnp.zeros((bsz, nh, dk, vc.shape[-1]), jnp.float32)
    oc_f, sc_f = gated_delta_chunked(qc, kc, vc, lac[0], bc[0], s0)
    ol_f, _ = gated_delta_chunked(ql, kl, vl, lal[0], bl[0], sc_f)
    r = lambda t: jnp.flip(t, axis=2)
    oc_b, sc_b = gated_delta_chunked(r(qc), r(kc), r(vc), r(lac[1]), r(bc[1]), s0)
    ol_b, _ = gated_delta_chunked(r(ql), r(kl), r(vl), r(lal[1]), r(bl[1]), sc_b)
    return oc_f + r(oc_b), ol_f + r(ol_b)

def gdn_output(o, z, norm_g):
    bsz, nh, t_len, dv = o.shape
    y = rms_norm(o.transpose(0, 2, 1, 3), norm_g) * jax.nn.silu(z.astype(jnp.float32).reshape(bsz, t_len, nh, dv))
    return y.reshape(bsz, t_len, nh * dv).astype(z.dtype)

def mla_heads(cq, ckv, kr, qn_g, kvn_g, w_uq, w_ukv, qk_g, rope):
    bsz, t_len, _ = cq.shape
    q = (rms_norm(cq, qn_g) @ w_uq).reshape(bsz, t_len, MLA_HEADS, MLA_NOPE + MLA_ROPE)
    kv = (rms_norm(ckv, kvn_g) @ w_ukv).reshape(bsz, t_len, MLA_HEADS, MLA_NOPE + MLA_V)
    k_nope, v = jnp.split(kv, [MLA_NOPE], axis=-1)
    q_nope = rms_norm(q[..., :MLA_NOPE], qk_g[0, :MLA_NOPE])
    q_pe = rms_norm(q[..., MLA_NOPE:], qk_g[0, MLA_NOPE:])
    k_nope = rms_norm(k_nope, qk_g[1, :MLA_NOPE])
    k_pe = rms_norm(kr[:, :, None, :], qk_g[1, MLA_NOPE:])
    if rope is not None:
        q_pe = apply_axial_rope(q_pe, rope)
        k_pe = apply_axial_rope(k_pe, rope)
    q = jnp.concatenate([q_nope, q_pe], axis=-1)
    k = jnp.concatenate([k_nope, jnp.broadcast_to(k_pe, (bsz, t_len, MLA_HEADS, MLA_ROPE))], axis=-1)
    return q, k, v

def gqa_heads(q, k, v, qk_g, rope):
    bsz, t_len, _ = q.shape
    q = rms_norm(q.reshape(bsz, t_len, -1, HEAD_DIM), qk_g[0])
    k = rms_norm(k.reshape(bsz, t_len, -1, HEAD_DIM), qk_g[1])
    v = v.reshape(bsz, t_len, -1, HEAD_DIM)
    if rope is not None:
        q = apply_axial_rope(q, rope)
        k = apply_axial_rope(k, rope)
    return q, k, v

def softmax_attend(q, k, v, scale, sink=None):
    bsz, tq, hq, d = q.shape
    hkv = k.shape[2]
    grp = hq // hkv
    dv = v.shape[-1]
    nb = tq // Q_BLOCK
    qb = q.reshape(bsz, nb, Q_BLOCK, hkv, grp, d).transpose(1, 0, 2, 3, 4, 5)

    def block(q_blk):
        s = jnp.einsum('bqhgd,bshd->bhgqs', q_blk, k, preferred_element_type=jnp.float32) * scale
        if sink is not None:
            s_sink = jnp.broadcast_to(sink.astype(jnp.float32).reshape(1, hkv, grp, 1, 1), s.shape[:-1] + (1,))
            p = jax.nn.softmax(jnp.concatenate([s, s_sink], axis=-1), axis=-1)[..., :-1]
        else:
            p = jax.nn.softmax(s, axis=-1)
        return jnp.einsum('bhgqs,bshd->bqhgd', p.astype(v.dtype), v)

    o = lax.map(block, qb)
    return o.transpose(1, 0, 2, 3, 4, 5).reshape(bsz, tq, hq, dv)

def banded_window_attention(q, k, v, k_ctx, v_ctx, sink, scale):
    bsz, t_len, hq, d = q.shape
    hkv = k.shape[2]
    grp = hq // hkv
    dv = v.shape[-1]
    w = WINDOW
    nb = t_len // w
    pad = ((0, 0), (w, w), (0, 0), (0, 0))
    kp = jnp.pad(k, pad)
    vp = jnp.pad(v, pad)
    kb = jnp.concatenate([kp[:, j * w:j * w + t_len].reshape(bsz, nb, w, hkv, d) for j in range(3)], axis=2)
    vb = jnp.concatenate([vp[:, j * w:j * w + t_len].reshape(bsz, nb, w, hkv, dv) for j in range(3)], axis=2)
    q_pos = jnp.arange(t_len).reshape(nb, w)
    k_pos = jnp.arange(nb)[:, None] * w + jnp.arange(3 * w)[None, :] - w
    valid = ((jnp.abs(q_pos[:, :, None] - k_pos[:, None, :]) <= w)
             & (k_pos >= 0)[:, None, :] & (k_pos < t_len)[:, None, :])
    qb = q.reshape(bsz, nb, w, hkv, grp, d)
    s_loc = jnp.einsum('bnqhgd,bnkhd->bnhgqk', qb, kb, preferred_element_type=jnp.float32) * scale
    s_loc = jnp.where(valid[None, :, None, None], s_loc, -jnp.inf)
    s_ctx = jnp.einsum('bnqhgd,bchd->bnhgqc', qb, k_ctx, preferred_element_type=jnp.float32) * scale
    s_sink = jnp.broadcast_to(sink.astype(jnp.float32).reshape(1, 1, hkv, grp, 1, 1), s_loc.shape[:-1] + (1,))
    p = jax.nn.softmax(jnp.concatenate([s_loc, s_ctx, s_sink], axis=-1), axis=-1)
    n_loc = 3 * w
    n_ctx = k_ctx.shape[1]
    o = (jnp.einsum('bnhgqk,bnkhd->bnqhgd', p[..., :n_loc].astype(v.dtype), vb)
         + jnp.einsum('bnhgqc,bchd->bnqhgd', p[..., n_loc:n_loc + n_ctx].astype(v.dtype), v_ctx))
    return o.reshape(bsz, t_len, hq, dv)

def token_mixers(pc, pl, conv_w, a_log, dt_bias, gdn_g, mla_qn_g, mla_kvn_g, w_uq, w_ukv, mla_qk_g,
                 swa_qk_g, swa_sink, gqa_qk_g, rope_hd, rope_mla, need_ctx):
    (aq_c, ak_c, av_c, az_c, aa_c, ab_c, mq_c, mkv_c, mkr_c, sq_c, sk_c, sv_c, gq_c, gk_c, gv_c) = pc
    (aq_l, ak_l, av_l, az_l, aa_l, ab_l, mq_l, mkv_l, mkr_l, sq_l, sk_l, sv_l, gq_l, gk_l, gv_l) = pl
    bsz, t_len, _ = aq_l.shape
    cat = lambda a, b: jnp.concatenate([a, b], axis=1)
    oa_c, oa_l = gdn_bidirectional(gdn_prepare(aq_c, ak_c, av_c, aa_c, ab_c, conv_w, a_log, dt_bias),
                                   gdn_prepare(aq_l, ak_l, av_l, aa_l, ab_l, conv_w, a_log, dt_bias))
    ya_l = gdn_output(oa_l, az_l, gdn_g)
    bq_c, bk_c, bv_c = mla_heads(mq_c, mkv_c, mkr_c, mla_qn_g, mla_kvn_g, w_uq, w_ukv, mla_qk_g, None)
    bq_l, bk_l, bv_l = mla_heads(mq_l, mkv_l, mkr_l, mla_qn_g, mla_kvn_g, w_uq, w_ukv, mla_qk_g, rope_mla)
    yb_l = softmax_attend(bq_l, cat(bk_c, bk_l), cat(bv_c, bv_l), MLA_SCALE)
    cq_c, ck_c, cv_c = gqa_heads(sq_c, sk_c, sv_c, swa_qk_g, None)
    cq_l, ck_l, cv_l = gqa_heads(sq_l, sk_l, sv_l, swa_qk_g, rope_hd)
    yc_l = banded_window_attention(cq_l, ck_l, cv_l, ck_c, cv_c, swa_sink, ATTN_SCALE)
    dq_c, dk_c, dv_c = gqa_heads(gq_c, gk_c, gv_c, gqa_qk_g, None)
    dq_l, dk_l, dv_l = gqa_heads(gq_l, gk_l, gv_l, gqa_qk_g, rope_hd)
    yd_l = softmax_attend(dq_l, cat(dk_c, dk_l), cat(dv_c, dv_l), ATTN_SCALE)
    mix_l = jnp.concatenate([ya_l, yb_l.reshape(bsz, t_len, -1), yc_l.reshape(bsz, t_len, -1),
                             yd_l.reshape(bsz, t_len, -1)], axis=-1)
    if not need_ctx:
        return None, mix_l
    n_ctx = aq_c.shape[1]
    ya_c = gdn_output(oa_c, az_c, gdn_g)
    yb_c = softmax_attend(bq_c, bk_c, bv_c, MLA_SCALE)
    yc_c = softmax_attend(cq_c, ck_c, cv_c, ATTN_SCALE, sink=swa_sink)
    yd_c = softmax_attend(dq_c, dk_c, dv_c, ATTN_SCALE)
    mix_c = jnp.concatenate([ya_c, yb_c.reshape(bsz, n_ctx, -1), yc_c.reshape(bsz, n_ctx, -1),
                             yd_c.reshape(bsz, n_ctx, -1)], axis=-1)
    return mix_c, mix_l

def moe_ffn(h, router_w, router_bias, w_gu, w_down, shared_gu, shared_down):
    n_tok, d = h.shape
    n_assign = n_tok * TOP_K
    scores = jax.nn.sigmoid(jnp.dot(h, router_w, preferred_element_type=jnp.float32))
    _, idx = lax.top_k(scores + router_bias.astype(jnp.float32), TOP_K)
    gates = jnp.take_along_axis(scores, idx, axis=-1)
    gates = gates / jnp.sum(gates, axis=-1, keepdims=True) * ROUTED_SCALE
    flat_e = idx.reshape(-1)
    order = jnp.argsort(flat_e)
    sorted_e = flat_e[order]
    counts = jnp.bincount(flat_e, length=N_EXPERTS)
    padded = (counts + MOE_BLOCK - 1) // MOE_BLOCK * MOE_BLOCK
    pad_end = jnp.cumsum(padded)
    run_start = jnp.cumsum(counts) - counts
    row = (pad_end - padded)[sorted_e] + jnp.arange(n_assign) - run_start[sorted_e]
    n_rows = -(-n_assign // MOE_BLOCK) * MOE_BLOCK + N_EXPERTS * MOE_BLOCK
    n_blk = n_rows // MOE_BLOCK
    src = jnp.full((n_rows,), n_tok, jnp.int32).at[row].set((order // TOP_K).astype(jnp.int32))
    row_gate = jnp.zeros((n_rows,), jnp.float32).at[row].set(gates.reshape(-1)[order])
    blk_expert = jnp.minimum(jnp.searchsorted(pad_end, jnp.arange(n_blk) * MOE_BLOCK, side='right'), N_EXPERTS - 1)
    h_pad = jnp.concatenate([h, jnp.zeros((1, d), h.dtype)], axis=0)

    def expert_block(args):
        src_b, gate_b, e = args
        y = swiglu(h_pad[src_b], w_gu[e], w_down[e])
        return y * gate_b[:, None].astype(y.dtype)

    y_rows = lax.map(expert_block, (src.reshape(n_blk, MOE_BLOCK), row_gate.reshape(n_blk, MOE_BLOCK), blk_expert))
    routed = jax.ops.segment_sum(y_rows.reshape(n_rows, d), src, num_segments=n_tok + 1)[:n_tok]
    return routed + swiglu(h, shared_gu, shared_down)

def setup_inputs(seed: int = 0) -> dict:
    key = jax.random.key(seed)
    keys = iter(jax.random.split(key, 40))
    f32 = jnp.float32
    L, D = DEPTH, D_MODEL

    def normal(shape, scale):
        return jax.random.normal(next(keys), shape, f32) * scale

    def gain(shape):
        return 1.0 + normal(shape, 0.05)

    a_log = jnp.log(jax.random.uniform(next(keys), (L, 2, GDN_HEADS), f32, 1.0, 16.0))
    dt = jnp.exp(jax.random.uniform(next(keys), (L, 2, GDN_HEADS), f32, math.log(1e-3), math.log(1e-1)))
    dt_bias = dt + jnp.log(-jnp.expm1(-dt))
    return {
        'x': normal((BATCH, SEQ, D), 1.0),
        'c': normal((BATCH, D), 1.0),
        'ctx': normal((BATCH, CTX_LEN, D), 1.0),
        'c_ctx': normal((D,), 1.0),
        'w_mod': normal((L, D, 6 * D), 0.5 * D ** -0.5),
        'b_mod': normal((L, 6 * D), 0.02),
        'norm1_g': gain((L, D)),
        'norm2_g': gain((L, D)),
        'w_in': normal((L, D, D_IN), D ** -0.5),
        'gdn_conv_w': normal((L, GDN_CONV, GDN_CONV_CH), GDN_CONV ** -0.5),
        'gdn_a_log': a_log,
        'gdn_dt_bias': dt_bias,
        'gdn_norm_g': gain((L, GDN_DV)),
        'mla_qn_g': gain((L, MLA_Q_RANK)),
        'mla_kvn_g': gain((L, MLA_KV_RANK)),
        'mla_w_uq': normal((L, MLA_Q_RANK, MLA_HEADS * (MLA_NOPE + MLA_ROPE)), MLA_Q_RANK ** -0.5),
        'mla_w_ukv': normal((L, MLA_KV_RANK, MLA_HEADS * (MLA_NOPE + MLA_V)), MLA_KV_RANK ** -0.5),
        'mla_qk_g': gain((L, 2, MLA_NOPE + MLA_ROPE)),
        'swa_qk_g': gain((L, 2, HEAD_DIM)),
        'swa_sink': normal((L, SWA_HEADS), 1.0),
        'gqa_qk_g': gain((L, 2, HEAD_DIM)),
        'w_out': normal((L, D_MIX, D), D_MIX ** -0.5),
        'router_w': normal((L, D, N_EXPERTS), D ** -0.5),
        'router_bias': normal((L, N_EXPERTS), 0.01),
        'exp_w_gu': normal((L, N_EXPERTS, D, 2 * D_EXPERT), D ** -0.5),
        'exp_w_down': normal((L, N_EXPERTS, D_EXPERT, D), D_EXPERT ** -0.5),
        'shared_w_gu': normal((L, D, 2 * D_EXPERT), D ** -0.5),
        'shared_w_down': normal((L, D_EXPERT, D), D_EXPERT ** -0.5),
    }

def reference(x, c, ctx, c_ctx, w_mod, b_mod, norm1_g, norm2_g, w_in, gdn_conv_w, gdn_a_log, gdn_dt_bias,
              gdn_norm_g, mla_qn_g, mla_kvn_g, mla_w_uq, mla_w_ukv, mla_qk_g, swa_qk_g, swa_sink, gqa_qk_g,
              w_out, router_w, router_bias, exp_w_gu, exp_w_down, shared_w_gu, shared_w_down):
    bsz, t_len, d = x.shape
    n_ctx = ctx.shape[1]
    n_rows = t_len // GRID_W
    rope_hd = axial_rope_tables(n_rows, HEAD_DIM)
    rope_mla = axial_rope_tables(n_rows, MLA_ROPE)
    silu_c = jax.nn.silu(c)
    silu_cc = jax.nn.silu(c_ctx)
    xl, xc = x, ctx
    for l in range(DEPTH):
        need_ctx = l < DEPTH - 1
        mod_l = jnp.split((silu_c @ w_mod[l] + b_mod[l])[:, None, :], 6, axis=-1)
        mod_c = jnp.split((silu_cc @ w_mod[l] + b_mod[l])[None, None, :], 6, axis=-1)
        hl = modulate(rms_norm(xl, norm1_g[l]), mod_l[0], mod_l[1])
        hc = modulate(rms_norm(xc, norm1_g[l]), mod_c[0], mod_c[1])
        mix_c, mix_l = token_mixers(
            split_columns(hc @ w_in[l]), split_columns(hl @ w_in[l]),
            gdn_conv_w[l], gdn_a_log[l], gdn_dt_bias[l], gdn_norm_g[l],
            mla_qn_g[l], mla_kvn_g[l], mla_w_uq[l], mla_w_ukv[l], mla_qk_g[l],
            swa_qk_g[l], swa_sink[l], gqa_qk_g[l], rope_hd, rope_mla, need_ctx)
        xl = xl + mod_l[2] * (mix_l @ w_out[l])
        hl = modulate(rms_norm(xl, norm2_g[l]), mod_l[3], mod_l[4])
        if need_ctx:
            xc = xc + mod_c[2] * (mix_c @ w_out[l])
            hc = modulate(rms_norm(xc, norm2_g[l]), mod_c[3], mod_c[4])
            y = moe_ffn(jnp.concatenate([hc, hl], axis=1).reshape(-1, d), router_w[l], router_bias[l],
                        exp_w_gu[l], exp_w_down[l], shared_w_gu[l], shared_w_down[l]).reshape(bsz, n_ctx + t_len, d)
            xc = xc + mod_c[5] * y[:, :n_ctx]
            xl = xl + mod_l[5] * y[:, n_ctx:]
        else:
            y = moe_ffn(hl.reshape(-1, d), router_w[l], router_bias[l], exp_w_gu[l], exp_w_down[l],
                        shared_w_gu[l], shared_w_down[l]).reshape(bsz, t_len, d)
            xl = xl + mod_l[5] * y
    return xl


_drawn_inputs = setup_inputs


def setup_inputs(seed=0):
    import zlib

    import numpy as np

    out = dict(_drawn_inputs(seed))
    spreads = {}
    factors = {'gdn_norm_g': 2.96,
     'mla_qn_g': 5.745,
     'mla_kvn_g': 3.493,
     'mla_qk_g': 6.674,
     'swa_qk_g': 4.214,
     'swa_sink': 64.0,
     'gqa_qk_g': 4.651}
    for name, (base, spread) in spreads.items():
        noise = np.random.default_rng([zlib.crc32(name.encode()), seed]).standard_normal(out[name].shape)
        drawn = base * np.exp(spread * noise) if base else spread * noise
        out[name] = jnp.asarray(drawn.astype(out[name].dtype))
    for name, factor in factors.items():
        out[name] = (out[name] * factor).astype(out[name].dtype)
    return out
```

```python
from contextlib import ExitStack

import numpy as np
import concourse.bass as bass
from concourse import mybir

P = 128
D = 1024
KD = D // P
DEPTH = 2
CTX = 256
SEQ = 256
GRID_W = 64
HEADS = 4
HD = 64
THETA = 10000.0
EPS = 1e-6
D_IN = 2480
QKV = 768
REST = D_IN - QKV
NCHUNK = 4
CW = REST // NCHUNK
CONV = 5
MLA_QR, MLA_KVR, MLA_NOPE, MLA_ROPE, MLA_V = 256, 128, 64, 32, 64
MLA_D = MLA_NOPE + MLA_ROPE
WINDOW = 128
NE = 64
TOPK = 6
CODES = 8
DE = 384
KE = DE // P
ROUTED = 2.5
NT = 4
MIX = 1024

C_Z, C_A, C_B, C_MQ, C_MKV, C_MKR = 0, 256, 264, 272, 528, 656
C_SQ, C_SV, C_GQ, C_GV = 688, 1072, 1200, 1584

F32 = mybir.dt.float32
I32 = mybir.dt.int32
U32 = mybir.dt.uint32
ALU = mybir.AluOpType
ACT = mybir.ActivationFunctionType
AX = mybir.AxisListType.X

CONST = {}
_at = 0
for _n, _w in (("ident", P), ("inc_f", P), ("inc_b", P), ("str_f", P), ("str_b", P), ("ones", P), ("b16", P),
               ("m32", P), ("m64", P), ("m128", P), ("window", 2 * SEQ), ("cos_hd", 2 * 6 * HD),
               ("sin_hd", 2 * 6 * HD), ("cos_pe", 2 * HEADS * MLA_ROPE), ("sin_pe", 2 * HEADS * MLA_ROPE),
               ("experts", NE)):
    CONST[_n] = (_at, _at + _w)
    _at += _w
N_CONST = _at
NO_CODE = 1 << 20


def rope_table(rot, copies):
    rows = np.repeat(np.arange(SEQ // GRID_W), GRID_W)
    cols = np.tile(np.arange(GRID_W), SEQ // GRID_W)
    axis = rot // 2
    freq = THETA ** (-np.arange(0, axis, 2) / axis)
    sign = np.concatenate([-np.ones(axis // 2), np.ones(axis // 2)] * 2)
    ang = np.concatenate([rows[:, None] * freq] * 2 + [cols[:, None] * freq] * 2, axis=1)
    return np.tile(np.cos(ang), copies), np.tile(np.sin(ang) * sign, copies)


def constants():
    a = np.zeros((P, N_CONST), np.float32)
    i, j = np.arange(P)[:, None], np.arange(P)[None, :]

    def put(name, value):
        lo, hi = CONST[name]
        a[:, lo:hi] = value

    put("ident", i == j)
    put("inc_f", i <= j)
    put("inc_b", i >= j)
    put("str_f", i > j)
    put("str_b", i < j)
    put("ones", np.ones((P, P)))
    put("b16", i // 16 == j // 16)
    for w in (32, 64, 128):
        put(f"m{w}", (i // w == j // w) & (i // (w // 2) != j // (w // 2)))
    q = np.arange(SEQ)[:, None]
    s = np.arange(SEQ)[None, :]
    far = np.where(np.abs(q - s) <= WINDOW, 0.0, -1e30)
    tiles = lambda t: t.reshape(2, P, -1).transpose(1, 0, 2).reshape(P, -1)
    put("window", tiles(far))
    cos, sin = rope_table(HD, 6)
    put("cos_hd", tiles(cos))
    put("sin_hd", tiles(sin))
    cos, sin = rope_table(MLA_ROPE, HEADS)
    put("cos_pe", tiles(cos))
    put("sin_pe", tiles(sin))
    put("experts", np.arange(NE)[None, :])
    return a


class Signal:

    def __init__(self, sem, steps, by=1, start=0):
        self.sem, self.by, self.start = sem, by, start
        self.base = [start + by * sum(steps[:u]) for u in range(len(steps))]

    def at(self, use, n):
        return self.base[use] + n * self.by


def build(nc, x, c, ctx, c_ctx, w_mod, b_mod, norm1_g, norm2_g, w_in, gdn_conv_w, gdn_a_log, gdn_dt_bias,
          gdn_norm_g, mla_qn_g, mla_kvn_g, mla_w_uq, mla_w_ukv, mla_qk_g, swa_qk_g, swa_sink, gqa_qk_g,
          w_out, router_w, router_bias, exp_w_gu, exp_w_down, shared_w_gu, shared_w_down, consts, out):
    with ExitStack() as stack:
        def sb(name, shape, dt=F32):
            return stack.enter_context(nc.sbuf_tensor(name, shape, dt))

        def dram(name, shape, dt=F32):
            return nc.dram_tensor(name, shape, dt, kind="Internal").ap()

        def sig(name, steps, by=1):
            return Signal(stack.enter_context(nc.semaphore(name)), steps, by)

        started = []

        def loop_sig(name, steps, by=1):
            started.append(Signal(stack.enter_context(nc.semaphore(name)), steps, by, start=by))
            return started[-1]

        OUT_TILES = [[0, 1, 2, 3]] * (DEPTH - 1) + [[2, 3]]
        ALL = [0, 1, 2, 3]
        NOUT = [len(t) for t in OUT_TILES]

        ps = [stack.enter_context(nc.psum_tensor(f"bank{i}", [P, 512], F32)) for i in range(8)]
        xs = sb("xs", [P, NT, D])
        hreg = sb("hreg", [P, NT * D])
        htreg = sb("htreg", [P, NT * D])
        modreg = sb("modreg", [P, 6 * D])
        const = sb("const", [P, N_CONST])
        A_WORDS = 27648
        arena = sb("arena", [P, A_WORDS])
        stat = sb("stat", [P, 512])

        def carve(reg, at, *dims, part=P, dt=None):
            n = int(np.prod(dims))
            v = reg[0:part, at:at + n]
            if dt is not None:
                v = v.bitcast(dt)
            names = "abcd"[:len(dims)]
            if len(dims) == 1:
                return v
            return v.rearrange(f"p ({' '.join(names)}) -> p {' '.join(names)}",
                               **{k: d for k, d in zip(names[1:], dims[1:])})

        def K(name, *dims):
            lo, hi = CONST[name]
            return carve(const, lo, *(dims or (hi - lo,)))

        ident = K("ident")
        ones = K("ones")
        h = carve(hreg, 0, NT, D)
        mix = h
        acc = h
        hT = carve(htreg, 0, KD, NT * P)
        mod = carve(modreg, 0, 3, 2, D)

        wmod = [carve(arena, 4096 * b, KD, 512) for b in range(3)]
        modrow = carve(arena, 12288, 6 * D, part=2)
        brow = carve(arena, 12288 + 6 * D, 6 * D, part=2)
        gains = carve(hreg, 0, 2, D, part=2)
        ccol = carve(stat, 0, 2, KD)
        scol = carve(stat, 32, 2, KD)

        pj = carve(arena, 0, NT, REST)
        conv_in = carve(arena, 6848, 6, 2, CTX + 4)
        conv_out = carve(arena, 9968, 6, NT * P)
        qkv = carve(arena, 13040, NT, QKV)
        qT = carve(arena, 16112, HEADS, NT * P, part=HD)
        kT = carve(arena, 18160, HEADS, NT * P, part=HD)
        win_qkv = carve(arena, 20208, KD, QKV)
        win = [carve(arena, 13040 + 3424 * b, KD, CW) for b in range(2)]
        convw = sb("convw", [P, 6, CONV])

        SM = {}
        sm_at = 0
        for n, w in (("a_log", 8), ("dt_bias", 8), ("gdn_g", HD), ("qn", MLA_QR), ("kvn", MLA_KVR), ("mla_qk", 2 * MLA_D),
                     ("swa_qk", 2 * HD), ("gqa_qk", 2 * HD), ("sink", HEADS), ("rbias", NE)):
            SM[n] = (sm_at, w)
            sm_at += w
        small = sb("small", [P, sm_at])
        srow = lambda n: small[:, SM[n][0]:SM[n][0] + SM[n][1]]
        small_src = {"a_log": lambda l: gdn_a_log[l].rearrange("a h -> (a h)"),
                     "dt_bias": lambda l: gdn_dt_bias[l].rearrange("a h -> (a h)"), "gdn_g": lambda l: gdn_norm_g[l],
                     "qn": lambda l: mla_qn_g[l], "kvn": lambda l: mla_kvn_g[l],
                     "mla_qk": lambda l: mla_qk_g[l].rearrange("a h -> (a h)"),
                     "swa_qk": lambda l: swa_qk_g[l].rearrange("a h -> (a h)"),
                     "gqa_qk": lambda l: gqa_qk_g[l].rearrange("a h -> (a h)"), "sink": lambda l: swa_sink[l],
                     "rbias": lambda l: router_bias[l]}
        N_SMALL = len(small_src)

        gm = [carve(arena, 20208 + 512 * i, HEADS, P) for i in range(14)]
        M_N, M_NT, M_PT, M_P, M_Z, M_QK, M_B32, M_B64, M_B128, M_E, M_ET, M_X, M_Y, M_L = gm
        gsq = carve(arena, 20208, NT, 512)
        gsum = carve(stat, 0, NT, 8)
        grs = carve(stat, 32, NT, 8)
        la = carve(stat, 64, NT, 8)
        beta = carve(stat, 96, NT, 8)
        gz = carve(stat, 128, NT, 8)
        ge = carve(stat, 160, NT, 8)
        gn = carve(stat, 192, 8)
        ecol = carve(stat, 208, 12)
        og = carve(arena, 6848, NT, HEADS * HD)
        S = carve(arena, 6848 + 1024, HEADS, HD, part=HD)
        vx = carve(arena, 6848 + 1280, HEADS, HD)
        vn = carve(arena, 6848 + 1536, HEADS, HD)
        vns = carve(arena, 6848 + 1792, HEADS, HD)
        osq = carve(arena, 9968, NT, 256)
        zs = carve(arena, 9968 + 1024, NT, 256)

        mq = carve(htreg, 0, NT, HEADS * MLA_D)
        mkv = carve(htreg, 1536, NT, HEADS * (MLA_NOPE + MLA_V))
        cT = carve(arena, 25328, 3, NT * P)
        mkf = carve(arena, 25328, NT, HEADS * MLA_D)
        wuq = carve(arena, 21232, 2, HEADS * MLA_D)
        wukv = carve(arena, 22000, HEADS * (MLA_NOPE + MLA_V))
        asq = carve(arena, 13040, NT, 512)
        asq2 = carve(arena, 15088, NT, 384)
        mqT = carve(arena, 21232, HEADS, NT * P, part=MLA_D)
        mkT = carve(arena, 23280, HEADS, NT * P, part=MLA_D)
        sqT = carve(arena, 6848, HEADS, NT * P, part=HD)
        skT = carve(arena, 8896, 2, NT * P, part=HD)
        gqT = carve(arena, 9968, HEADS, NT * P, part=HD)
        gkT = carve(arena, 12016, 2, NT * P, part=HD)
        prob = [carve(arena, 25328 + 512 * b, 512) for b in range(2)]
        probT = [carve(arena, 26352 + 512 * b, 4, P) for b in range(2)]
        wout = carve(arena, 13040, KD, D)
        mixT = hT
        asum = carve(stat, 224, 128)
        arow = carve(stat, 352, 4, 8)
        tmp_o = carve(arena, 21232, 512)

        wgu = [carve(arena, 9216 * b, KD, 2 * DE) for b in range(2)]
        wdn = [carve(arena, 9216 * b + 6144, KE, D) for b in range(2)]
        sgu = carve(arena, 18432, KD, 2 * DE)
        sdn = carve(arena, 18432 + 6144, KE, D)
        rw = sb("rw", [P, KD, NE])
        onehot = [carve(arena, 384 * i, TOPK, NE) for i in range(NT)]
        ohp = carve(arena, 1536, TOPK, NE)
        scores = carve(arena, 2048, NT, NE)
        sel = carve(arena, 2304, NT, NE)
        mask = carve(arena, 2560, NT, NE)
        pos = carve(arena, 2816, NT, NE)
        top8 = carve(arena, 3072, NT, 8)
        idx8 = carve(arena, 3104, NT, 8, dt=U32)
        idxf = carve(arena, 3136, NT, 8)
        gate = sb("gate", [P, NT, 8])
        gatesum = carve(arena, 3168, NT)
        posk = carve(arena, 3200, NT, 8)
        addr = carve(arena, 3232, NT, 8, dt=U32)
        code = carve(arena, 3264, NT, 8, dt=U32)
        nocode = carve(arena, 3328, 4 * NE, dt=U32)
        cntmax = carve(arena, 3600, 8)
        maxcnt = sb("maxcnt", [1, 8], I32)
        RING = 4
        AHEAD = RING - 1
        NL = NE + AHEAD + 1
        lst = sb("lst", [P, NT, NL], U32)
        lsg = sb("lsg", [P, NT, NL], U32)
        gidx = sb("gidx", [P, RING, 1], U32)
        sidx = sb("sidx", [P, RING, 1], U32)
        hg = [carve(arena, 18432 + 1024 * b, D) for b in range(RING)]
        hgT = [carve(htreg, 1024 * b, KD, P) for b in range(2)]
        yo = [carve(arena, 22528 + 1024 * b, D) for b in range(RING)]
        sgb = carve(modreg, 2048, DE)
        act_ = carve(modreg, 2048 + DE, DE)
        actT = carve(modreg, 2048 + 2 * DE, KE, P)
        yrow = [carve(arena, 6144 * b, TOPK, D) for b in range(2)]

        mod_d = dram("mod_d", [DEPTH, 2, 6 * D])
        h_d = dram("h_d", [NT * P, D])
        list_d = dram("list_d", [NT * P * NE, 1], U32)
        y_d = dram("y_d", [NT * P * CODES, D])

        LAYERS = range(DEPTH)
        one = [1] * DEPTH
        U = 2 * DEPTH
        n_norm = [NT if u % 2 == 0 else NOUT[u // 2] for u in range(U)]
        phase_done = sig("phase_done", [1])
        dve_step = stack.enter_context(nc.semaphore("dve_step"))
        pool_go = stack.enter_context(nc.semaphore("pool_go"))
        pool_step = stack.enter_context(nc.semaphore("pool_step"))

        start_loaded = sig("start_loaded", [3], 16)
        cond_loaded = sig("cond_loaded", [2], 16)
        cond_silu = sig("cond_silu", [1])
        wmod_loaded = [sig(f"wmod_loaded{b}", [4 * DEPTH], 16) for b in range(3)]
        modb_loaded = sig("modb_loaded", [6] * DEPTH, 16)
        modp_psum = sig("modp_psum", [12 * DEPTH])
        modrow_part = sig("modrow_part", [12 * DEPTH])
        modrow_ready = sig("modrow_ready", one)
        modrow_stored = sig("modrow_stored", one, 16)

        mod_loaded = sig("mod_loaded", [6] * U, 16)
        squares_ready = sig("squares_ready", n_norm)
        meansq_ready = sig("meansq_ready", [1] * U)
        std_ready = sig("std_ready", [1] * U)
        h_ready = sig("h_ready", n_norm)
        hT_psum = sig("hT_psum", [2 * n for n in n_norm])
        hT_ready = sig("hT_ready", [2 * n for n in n_norm])

        small_loaded = sig("small_loaded", [N_SMALL + 6] * DEPTH, 16)
        winq_loaded = sig("winq_loaded", one, 16)
        win_loaded = [sig(f"win_loaded{b}", [NCHUNK // 2] * DEPTH, 16) for b in range(2)]
        pads_ready = sig("pads_ready", [2] * DEPTH)
        qkvT_psum = sig("qkvT_psum", [6] * DEPTH)
        qkvT_ready = sig("qkvT_ready", [6] * DEPTH)
        conv_ready = sig("conv_ready", [6] * DEPTH)
        conv_silu = sig("conv_silu", [6] * DEPTH)
        proj_psum = sig("proj_psum", [NCHUNK * NT] * DEPTH)
        proj_ready = sig("proj_ready", [NCHUNK * NT] * DEPTH)
        tok_psum = sig("tok_psum", [2 * NT] * DEPTH)
        tok_ready = sig("tok_ready", [2 * NT] * DEPTH)

        gate_in = sig("gate_in", [2] * DEPTH)
        gate_act = sig("gate_act", [4] * DEPTH)
        qk_meansq = sig("qk_meansq", one)
        qk_std = sig("qk_std", one)
        qk_normed = sig("qk_normed", one)
        qkT_psum = sig("qkT_psum", [2 * NT] * DEPTH)
        qkT_ready = sig("qkT_ready", [2 * NT] * DEPTH)

        class Steps:

            def __init__(self, name, steps):
                self.steps = steps
                self.counter = sig(name, [len(steps) * NB] * DEPTH)
                self.sem = self.counter.sem

            def after(self, l, b, s):
                return self.counter.at(l, b * len(self.steps) + self.steps.index(s) + 1)

        NB = 2 * NT
        g_pe = Steps("gdn_pe", ["sums", "decay", "decayT", "kk", "kq", "aT", "n2", "n2T", "p1", "n4", "n4T", "p2", "n8",
                                "p3", "P32", "z32", "pz32", "P64", "z64", "pz64", "P128", "z128", "pz128", "ks",
                                "vn", "o", "s"])
        g_dve = Steps("gdn_dve", ["decay_in", "a", "n", "b", "qk", "pt0", "pt1", "pt2", "pt3", "pt32", "pt64", "pt128",
                                  "x", "vns", "out"])
        g_act = Steps("gdn_act", ["sums", "decay", "decayT", "n2", "n2T", "n4", "n4T", "n8", "P32", "z32", "P64", "z64",
                                  "P128", "z128", "vn"])
        state_zero = sig("state_zero", [2] * DEPTH)

        lat_meansq = sig("lat_meansq", one)
        lat_std = sig("lat_std", [2] * DEPTH)
        lat_ready = sig("lat_ready", one)
        up_loaded = sig("up_loaded", [2] * DEPTH, 16)
        cT_psum = sig("cT_psum", [NT] * DEPTH)
        cT_ready = sig("cT_ready", [NT] * DEPTH)
        up_psum = sig("up_psum", [2 * NT] * DEPTH)
        upq_ready = sig("upq_ready", [NT] * DEPTH)
        upkv_ready = sig("upkv_ready", [NT] * DEPTH)
        hd_meansq = sig("hd_meansq", one)
        hd_std = sig("hd_std", one)
        heads_ready = sig("heads_ready", one)
        hdT_psum = sig("hdT_psum", [6 * NT] * DEPTH)
        hdT_ready = sig("hdT_ready", [6 * NT] * DEPTH)

        units = [[(m, hh, t) for m in ("mla", "swa", "gqa") for hh in range(HEADS) for t in OUT_TILES[l]] for l in LAYERS]
        NU = [len(u) for u in units]
        scores_psum = sig("scores_psum", NU)
        negmax_ready = sig("negmax_ready", NU)
        probs_ready = sig("probs_ready", NU)
        sink_ready = sig("sink_ready", [n // 3 for n in NU])
        probT_psum = sig("probT_psum", NU)
        probT_ready = sig("probT_ready", NU)
        value_psum = sig("value_psum", NU)
        head_done = sig("head_done", NU)

        wout_loaded = sig("wout_loaded", one, 16)
        mixT_psum = sig("mixT_psum", [2 * n for n in NOUT])
        mixT_ready = sig("mixT_ready", [2 * n for n in NOUT])
        out_psum = sig("out_psum", [2 * n for n in NOUT])
        resid_ready = sig("resid_ready", [2 * n for n in NOUT])

        h_stored = sig("h_stored", NOUT, 16)
        router_loaded = sig("router_loaded", one, 16)
        shared_loaded = sig("shared_loaded", [2] * DEPTH, 16)
        router_psum = sig("router_psum", one)
        sigmoid_ready = sig("sigmoid_ready", one)
        mask_ready = sig("mask_ready", one)
        pos_psum = sig("pos_psum", one)
        nocode_ready = sig("nocode_ready", one)
        lists_cleared = sig("lists_cleared", one, 16)
        code_ready = sig("code_ready", one)
        addr_ready = sig("addr_ready", one)
        listed = sig("listed", [TOPK * n for n in NOUT], 16)
        tail_ready = sig("tail_ready", one)
        lists_loaded = sig("lists_loaded", one, 16)
        sh_gu = sig("shared_gu_psum", NOUT)
        sh_silu = sig("shared_silu", NOUT)
        sh_act = sig("shared_act", NOUT)
        sh_aT_psum = sig("shared_actT_psum", NOUT)
        sh_aT = sig("shared_actT", NOUT)
        sh_dn = sig("shared_down_psum", NOUT)
        sh_y = sig("shared_y", [2 * n for n in NOUT])

        R = NOUT
        EX = {}
        for kind, steps, extra in (("first", [NE] * DEPTH, 1), ("more", [NE * (r - 1) for r in R], 0)):
            more = [s + extra for s in steps]
            asked = [s + AHEAD * extra for s in steps]
            EX[kind] = dict(
                w=[loop_sig(f"{kind}_weights_loaded{b}", [s // 2 for s in steps], 32) for b in range(2)],
                g_idx=loop_sig(f"{kind}_gather_idx", asked), hT_psum=loop_sig(f"{kind}_slotT_psum", more),
                hT=loop_sig(f"{kind}_slotT", more), gu=loop_sig(f"{kind}_gu_psum", steps),
                silu=loop_sig(f"{kind}_silu", steps), act=loop_sig(f"{kind}_act", steps),
                aT_psum=loop_sig(f"{kind}_actT_psum", steps), aT=loop_sig(f"{kind}_actT", steps),
                dn=loop_sig(f"{kind}_down_psum", steps), y=loop_sig(f"{kind}_y", [2 * s for s in steps]),
                s_idx=loop_sig(f"{kind}_scatter_idx", steps), serial=False)
        EX["first"]["gathered"] = [loop_sig(f"first_gathered{b}", [(NE + AHEAD + RING - 1 - b) // RING] * DEPTH, 16)
                                   for b in range(RING)]
        EX["first"]["scattered"] = [loop_sig(f"first_scattered{b}", [NE // RING] * DEPTH, 16) for b in range(RING)]
        for l in LAYERS:
            steps = [NE * (r - 1) * (j == l) for j, r in enumerate(R)]
            EX[f"more{l}"] = dict(EX["more"], serial=True, gathered=[loop_sig(f"more{l}_gathered", steps, 16)] * RING,
                                  scattered=[loop_sig(f"more{l}_scattered", steps, 16)] * RING)
        del EX["more"]

        def uses(X, n, m):
            return n if X["serial"] else m

        yrow_loaded = [sig(f"yrow_loaded{b}", [n // 2 for n in NOUT], 16) for b in range(2)]
        y_added = sig("y_added", NOUT)
        out_stored = sig("out_stored", [2], 16)

        phases = {}

        def phase_end(eng, name):
            n = phases[name] = phases.get(name, 0) + 1
            eng.drain().then_inc(phase_done.sem, 1)
            eng.wait_ge(phase_done.sem, 5 * n)

        def bc(ap, at, n):
            v = ap.unsqueeze(at)
            shape = list(v.shape)
            shape[at] = n
            return v.broadcast_to(shape)

        def heads4(ap, d=HD):
            if len(ap.shape) == 2:
                return ap.rearrange("p (g d) -> p g d", d=d)
            return ap.rearrange("p t (g d) -> p t g d", d=d)

        tok = lambda t: slice(t * P, (t + 1) * P)

        def more_slots(eng, l, body, gives):
            big = eng.value_load(maxcnt[0:1, 0:1], min_val=0, max_val=NT * P)
            with eng.If(big > P):
                with eng.Fori(1, R[l]) as r:
                    with eng.Fori(0, NE // RING) as i:
                        for b in range(RING):
                            body(EX[f"more{l}"], l, r, RING * i + b, r * NE + RING * i + (b - NE),
                                 r * (NE // RING) + i - NE // RING, b)
                if eng is nc.gpsimd:
                    done = EX[f"more{l}"]["scattered"][0]
                    eng.wait_ge(done.sem, done.at(l, NE * (R[l] - 1)))
            with eng.Else():
                for name in gives:
                    for one_of in EX[f"more{l}"][name] if name == "w" else [EX[f"more{l}"][name]]:
                        steps = NE * (R[l] - 1) * (2 if name == "y" else 1) // (2 if name == "w" else 1)
                        eng.sem_inc(one_of.sem, (steps // 2 if name == "y" else steps) * one_of.by)
            eng.nop()

        block = stack.enter_context(nc.Block())

        @block.sync
        def _(sp):
            sp.dma_start(const[:], consts).then_inc(start_loaded.sem, 16)
            sp.dma_start(xs[:, 0:2, :], ctx.rearrange("a (t p) d -> p (a t) d", p=P)).then_inc(start_loaded.sem, 16)
            sp.dma_start(xs[:, 2:4, :], x.rearrange("a (t p) d -> p (a t) d", p=P)).then_inc(start_loaded.sem, 16)
            with nc.allow_non_contiguous_dma(reason="conditioning vectors as columns"):
                sp.dma_start(ccol[:, 0, :], c_ctx.rearrange("(k p) -> p k", p=P)).then_inc(cond_loaded.sem, 16)
                sp.dma_start(ccol[:, 1, :], c.rearrange("a (k p) -> p (a k)", p=P)).then_inc(cond_loaded.sem, 16)
            for l in LAYERS:
                if l:
                    sp.wait_ge(modrow_stored.sem, modrow_stored.at(l - 1, 1))
                for s in range(2):
                    sp.dma_start(brow[s:s + 1, :], b_mod[l:l + 1, :]).then_inc(modb_loaded.sem, 16)
                    sp.dma_start(gains[s:s + 1, 0, :], norm1_g[l:l + 1, :]).then_inc(modb_loaded.sem, 16)
                    sp.dma_start(gains[s:s + 1, 1, :], norm2_g[l:l + 1, :]).then_inc(modb_loaded.sem, 16)
                for j in range(12):
                    n = 12 * l + j
                    if n >= 3:
                        sp.wait_ge(modp_psum.sem, n - 2)
                    sp.dma_start(wmod[n % 3], w_mod[l].rearrange("(k p) n -> p k n", p=P)[:, :, 512 * j:512 * j + 512]
                                 ).then_inc(wmod_loaded[n % 3].sem, 16)
                sp.wait_ge(modrow_ready.sem, modrow_ready.at(l, 1))
                sp.dma_start(mod_d[l], modrow).then_inc(modrow_stored.sem, 16)
            sp.wait_ge(modrow_stored.sem, modrow_stored.at(DEPTH - 1, 1))
            phase_end(sp, "sp")

            def load_mod(l, half):
                for i in range(3):
                    for s in range(2):
                        j = 3 * half + i
                        sp.dma_start(mod[:, i, s, :], mod_d[l, s:s + 1, j * D:(j + 1) * D].broadcast_to([P, D])
                                     ).then_inc(mod_loaded.sem, 16)

            def load_projection(l):
                wv = w_in[l].rearrange("(k p) n -> p k n", p=P)
                sp.dma_start(win_qkv, wv[:, :, 0:QKV]).then_inc(winq_loaded.sem, 16)
                for b in range(2):
                    sp.dma_start(win[b], wv[:, :, QKV + b * CW:QKV + (b + 1) * CW]).then_inc(win_loaded[b].sem, 16)

            for l in LAYERS:
                load_mod(l, 0)
                wv = w_in[l].rearrange("(k p) n -> p k n", p=P)
                if l == 0:
                    load_projection(l)
                for n, src in small_src.items():
                    sp.dma_start(srow(n), src(l).unsqueeze(0).broadcast_to([P, SM[n][1]])).then_inc(small_loaded.sem, 16)
                with nc.allow_non_contiguous_dma(reason="taps as columns"):
                    for ct in range(6):
                        sp.dma_start(convw[:, ct, :], gdn_conv_w[l, :, tok(ct)].rearrange("j p -> p j")
                                     ).then_inc(small_loaded.sem, 16)
                phase_end(sp, "sp")
                for ch in range(2, NCHUNK):
                    sp.wait_ge(proj_psum.sem, proj_psum.at(l, NT * (ch - 1)))
                    sp.dma_start(win[ch % 2], wv[:, :, QKV + ch * CW:QKV + (ch + 1) * CW]
                                 ).then_inc(win_loaded[ch % 2].sem, 16)
                phase_end(sp, "sp")
                phase_end(sp, "sp")
                phase_end(sp, "sp")
                sp.dma_start(wuq, mla_w_uq[l].rearrange("(k p) n -> p k n", p=P)).then_inc(up_loaded.sem, 16)
                sp.dma_start(wukv, mla_w_ukv[l]).then_inc(up_loaded.sem, 16)
                phase_end(sp, "sp")
                phase_end(sp, "sp")
                sp.dma_start(wout, w_out[l].rearrange("(k p) n -> p k n", p=P)).then_inc(wout_loaded.sem, 16)
                phase_end(sp, "sp")
                phase_end(sp, "sp")
                load_mod(l, 1)
                sp.dma_start(rw[:], router_w[l].rearrange("(k p) n -> p k n", p=P)).then_inc(router_loaded.sem, 16)
                sp.dma_start(sgu, shared_w_gu[l].rearrange("(k p) n -> p k n", p=P)).then_inc(shared_loaded.sem, 16)
                sp.dma_start(sdn, shared_w_down[l].rearrange("(k p) n -> p k n", p=P)).then_inc(shared_loaded.sem, 16)
                for i, t in enumerate(OUT_TILES[l]):
                    sp.wait_ge(h_ready.sem, h_ready.at(2 * l + 1, i + 1))
                    sp.dma_start(h_d[tok(i), :], h[:, t, :]).then_inc(h_stored.sem, 16)
                sp.wait_ge(h_stored.sem, h_stored.at(l, NOUT[l]))
                phase_end(sp, "sp")
                X = EX["first"]
                sp.dma_start(wgu[1], exp_w_gu[l, 1].rearrange("(k p) n -> p k n", p=P)).then_inc(X["w"][1].sem, 16)
                for b in range(2):
                    sp.dma_start(wdn[b], exp_w_down[l, b].rearrange("(k p) n -> p k n", p=P)).then_inc(X["w"][b].sem, 16)
                sp.wait_ge(nocode_ready.sem, nocode_ready.at(l, 1))
                sp.dma_start(list_d.rearrange("(p a) b -> p (a b)", p=P), nocode).then_inc(lists_cleared.sem, 16)
                sp.wait_ge(listed.sem, listed.at(l, TOPK * NOUT[l]))
                sp.dma_start(lst[:, 0:R[l], 0:NE], list_d.rearrange("(r s e) b -> s r (e b)", s=P, e=NE)[:, 0:R[l], :]
                             ).then_inc(lists_loaded.sem, 16)
                phase_end(sp, "sp")

                def load_expert(X, e, b):
                    sp.dma_start(wgu[b], exp_w_gu[l, bass.ds(e, 1)].rearrange("e (k p) n -> p (e k) n", p=P)
                                 ).then_inc(X["w"][b].sem, 16)
                    sp.dma_start(wdn[b], exp_w_down[l, bass.ds(e, 1)].rearrange("e (k p) n -> p (e k) n", p=P)
                                 ).then_inc(X["w"][b].sem, 16)

                X = EX["first"]
                sp.dma_start(wgu[0], exp_w_gu[l, 0].rearrange("(k p) n -> p k n", p=P)).then_inc(X["w"][0].sem, 16)
                with sp.Fori(1, NE // 2) as i:
                    for b in range(2):
                        sp.wait_ge(X["dn"].sem, X["dn"].at(l, 2 * i + (b - 1)))
                        load_expert(X, 2 * i + b, b)
                phase_end(sp, "sp")

                def load_more(X, l, r, e, n, m, b):
                    sp.wait_ge(X["dn"].sem, X["dn"].at(l, n))
                    load_expert(X, e, b % 2)

                more_slots(sp, l, load_more, ["w"])
                phase_end(sp, "sp")
                for i in range(NOUT[l]):
                    if i >= 2:
                        sp.wait_ge(y_added.sem, y_added.at(l, i - 1))
                    if i == 2 or NOUT[l] == 2 and i == 1:
                        if l + 1 < DEPTH:
                            load_projection(l + 1)
                    sp.dma_start(yrow[i % 2], y_d.rearrange("(t p k) d -> t p k d", p=P, k=CODES)[i, :, 0:TOPK, :]
                                 ).then_inc(yrow_loaded[i % 2].sem, 16)
                phase_end(sp, "sp")
            for i in range(2):
                sp.dma_start(out[0, tok(i), :], xs[:, 2 + i, :]).then_inc(out_stored.sem, 16)
            sp.wait_ge(out_stored.sem, 32)

        @block.tensor
        def _(pe):
            mm = pe.matmul
            pe.wait_ge(cond_silu.sem, 1)
            for n in range(12 * DEPTH):
                pe.wait_ge(wmod_loaded[n % 3].sem, 16 * (n // 3 + 1))
                if n >= 2:
                    pe.wait_ge(modrow_part.sem, n - 1)
                for k in range(KD):
                    last = mm(ps[n % 2][0:2, :], scol[:, :, k], wmod[n % 3][:, k, :], start=(k == 0), stop=(k == KD - 1))
                last.then_inc(modp_psum.sem, 1)
            pe.wait_ge(start_loaded.sem, 48)
            phase_end(pe, "pe")

            def norm(u, tiles):
                for i, t in enumerate(tiles):
                    pe.wait_ge(h_ready.sem, h_ready.at(u, i + 1))
                    for half in range(2):
                        n = 2 * i + half
                        if n >= 4:
                            pe.wait_ge(hT_ready.sem, hT_ready.at(u, n - 3))
                        for k in range(4):
                            last = pe.transpose(ps[n % 4][:, tok(k)], h[:, t, tok(4 * half + k)], ident)
                        last.then_inc(hT_psum.sem, 1)

            def up_norm(l):
                for t in range(NT):
                    if t == 0:
                        pe.wait_ge(lat_ready.sem, lat_ready.at(l, 1))
                    if t >= 2:
                        pe.wait_ge(cT_ready.sem, cT_ready.at(l, t - 1))
                    for k in range(3):
                        last = pe.transpose(ps[t % 2][:, tok(k)], pj[:, t, C_MQ + k * P:C_MQ + (k + 1) * P], ident)
                    last.then_inc(cT_psum.sem, 1)
                pe.wait_ge(up_loaded.sem, up_loaded.at(l, 2))
                for t in range(NT):
                    pe.wait_ge(cT_ready.sem, cT_ready.at(l, t + 1))
                    if t >= 2:
                        pe.wait_ge(upq_ready.sem, upq_ready.at(l, t - 1))
                    for k in range(2):
                        last = mm(ps[2 + t % 2][:, 0:HEADS * MLA_D], cT[:, k, tok(t)], wuq[:, k, :],
                                  start=(k == 0), stop=(k == 1))
                    last.then_inc(up_psum.sem, 1)
                    if t >= 2:
                        pe.wait_ge(upkv_ready.sem, upkv_ready.at(l, t - 1))
                    mm(ps[4 + t % 2][:], cT[:, 2, tok(t)], wukv, start=True, stop=True).then_inc(up_psum.sem, 1)

            for l in LAYERS:
                norm(2 * l, ALL)
                phase_end(pe, "pe")
                pe.wait_ge(winq_loaded.sem, winq_loaded.at(l, 1))
                for ct in range(6):
                    if ct >= 2:
                        pe.wait_ge(qkvT_ready.sem, qkvT_ready.at(l, ct - 1))
                    for k in range(KD):
                        last = mm(ps[ct % 2][:], win_qkv[:, k, tok(ct)], hT[:, k, :], start=(k == 0), stop=(k == KD - 1))
                    last.then_inc(qkvT_psum.sem, 1)
                for ch in range(NCHUNK):
                    pe.wait_ge(win_loaded[ch % 2].sem, win_loaded[ch % 2].at(l, ch // 2 + 1))
                    for t in range(NT):
                        n = NT * ch + t
                        if n >= 4:
                            pe.wait_ge(proj_ready.sem, proj_ready.at(l, n - 3))
                        for k in range(KD):
                            last = mm(ps[2 + n % 4][:, 0:CW], hT[:, k, tok(t)], win[ch % 2][:, k, :],
                                      start=(k == 0), stop=(k == KD - 1))
                        last.then_inc(proj_psum.sem, 1)
                pe.wait_ge(conv_silu.sem, conv_silu.at(l, 6))
                pe.wait_ge(proj_psum.sem, proj_psum.at(l, NCHUNK * NT))
                for n in range(2 * NT):
                    t, half = divmod(n, 2)
                    if n >= 2:
                        pe.wait_ge(tok_ready.sem, tok_ready.at(l, n - 1))
                    for j in range(3):
                        last = pe.transpose(ps[n % 2][:, tok(j)], conv_out[:, 3 * half + j, tok(t)], ident)
                    last.then_inc(tok_psum.sem, 1)
                phase_end(pe, "pe")
                pe.wait_ge(qk_normed.sem, qk_normed.at(l, 1))
                for n in range(2 * NT):
                    t, which = divmod(n, 2)
                    if n >= 2:
                        pe.wait_ge(qkT_ready.sem, qkT_ready.at(l, n - 1))
                    for hh in range(HEADS):
                        g = which * HEADS + hh
                        last = pe.transpose(ps[n % 2][0:HD, tok(hh)], qkv[:, t, g * HD:(g + 1) * HD], ident)
                    last.then_inc(qkT_psum.sem, 1)
                phase_end(pe, "pe")

                for b in range(NB):
                    d, t = divmod(b, NT)
                    if d:
                        t = (1, 0, 3, 2)[t]
                    inc, strict = K("inc_b" if d else "inc_f"), K("str_b" if d else "str_f")

                    def done(ins):
                        ins.then_inc(g_pe.sem, 1)

                    def four(bank, lhs, rhs, w=P, rows=P, at=0):
                        for hh in range(HEADS):
                            last = mm(ps[bank][0:rows, at + hh * w:at + (hh + 1) * w], lhs(hh), rhs(hh), start=True, stop=True)
                        return last

                    if b:
                        pe.wait_ge(g_dve.sem, g_dve.after(l, b - 1, "out"))
                    lat = la[:, t, HEADS * d:HEADS * d + HEADS]
                    mm(ps[7][:, 0:4], inc, lat, start=True, stop=True)
                    mm(ps[7][:, 4:8], strict, lat, start=True, stop=True)
                    done(mm(ps[7][:, 8:12], ones, lat, start=True, stop=True))
                    pe.wait_ge(g_dve.sem, g_dve.after(l, b, "decay_in"))
                    done(mm(ps[0][:], inc, M_X.rearrange("p h j -> p (h j)"), start=True, stop=True))
                    done(mm(ps[1][:], strict, M_Y.rearrange("p h j -> p (h j)"), start=True, stop=True))
                    done(four(2, lambda q: kT[:, q, tok(t)], lambda q: kT[:, q, tok(t)]))
                    done(four(3, lambda q: kT[:, q, tok(t)], lambda q: qT[:, q, tok(t)]))
                    pe.wait_ge(g_dve.sem, g_dve.after(l, b, "a"))
                    for hh in range(HEADS):
                        last = pe.transpose(ps[4][:, tok(hh)], M_L[:, hh, :], ident)
                    done(last)
                    pe.wait_ge(g_dve.sem, g_dve.after(l, b, "pt0"))
                    done(four(5, lambda q: M_NT[:, q, :], lambda q: M_N[:, q, :]))
                    done(four(6, lambda q: M_N[:, q, :], lambda q: M_NT[:, q, :]))
                    pe.wait_ge(g_act.sem, g_act.after(l, b, "n2"))
                    done(four(4, lambda q: M_Z[:, q, :], lambda q: M_PT[:, q, :]))
                    pe.wait_ge(g_act.sem, g_act.after(l, b, "n2T"))
                    done(four(5, lambda q: M_P[:, q, :], lambda q: M_Z[:, q, :]))
                    done(four(6, lambda q: M_Z[:, q, :], lambda q: M_P[:, q, :]))
                    pe.wait_ge(g_act.sem, g_act.after(l, b, "n4"))
                    pe.wait_ge(g_dve.sem, g_dve.after(l, b, "pt1"))
                    done(four(4, lambda q: M_N[:, q, :], lambda q: M_PT[:, q, :]))
                    pe.wait_ge(g_act.sem, g_act.after(l, b, "n4T"))
                    done(four(5, lambda q: M_NT[:, q, :], lambda q: M_N[:, q, :]))
                    pe.wait_ge(g_act.sem, g_act.after(l, b, "n8"))
                    pe.wait_ge(g_dve.sem, g_dve.after(l, b, "pt2"))
                    done(four(4, lambda q: M_Z[:, q, :], lambda q: M_PT[:, q, :]))
                    for w, B, was in (("32", M_B32, "pt3"), ("64", M_B64, "pt32"), ("128", M_B128, "pt64")):
                        pe.wait_ge(g_dve.sem, g_dve.after(l, b, was))
                        for hh in range(HEADS):
                            last = pe.transpose(ps[5][:, tok(hh)], M_PT[:, hh, :], ident)
                        done(last)
                        done(four(6, lambda q: B[:, q, :], lambda q: M_PT[:, q, :]))
                        pe.wait_ge(g_act.sem, g_act.after(l, b, "z" + w))
                        done(four(4, lambda q: M_P[:, q, :], lambda q: M_Z[:, q, :]))
                    if b % NT == 0:
                        pe.wait_ge(state_zero.sem, state_zero.at(l, d + 1))
                    four(0, lambda q: kT[:, q, tok(t)], lambda q: S[:, q, :], HD)
                    done(four(0, lambda q: qT[:, q, tok(t)], lambda q: S[:, q, :], HD, at=HEADS * HD))
                    pe.wait_ge(g_dve.sem, g_dve.after(l, b, "x"))
                    done(four(1, lambda q: M_PT[:, q, :], lambda q: vx[:, q, :], HD))
                    pe.wait_ge(g_act.sem, g_act.after(l, b, "vn"))
                    pe.wait_ge(g_dve.sem, g_dve.after(l, b, "vns"))
                    done(four(2, lambda q: M_QK[:, q, :], lambda q: vn[:, q, :], HD))
                    done(four(3, lambda q: qkv[:, t, 256 + q * HD:256 + (q + 1) * HD], lambda q: vns[:, q, :], HD, rows=HD))
                phase_end(pe, "pe")
                up_norm(l)
                phase_end(pe, "pe")

                pe.wait_ge(heads_ready.sem, heads_ready.at(l, 1))
                for t in range(NT):
                    for j, (src, n_h, d) in enumerate(((mq, 4, MLA_D), (mkf, 4, MLA_D), (C_SQ, 4, HD), (C_SQ + 256, 2, HD),
                                                       (C_GQ, 4, HD), (C_GQ + 256, 2, HD))):
                        n = 6 * t + j
                        if n >= 4:
                            pe.wait_ge(hdT_ready.sem, hdT_ready.at(l, n - 3))
                        for q in range(n_h):
                            a = pj[:, t, src + q * d:src + (q + 1) * d] if isinstance(src, int) else src[:, t, q * d:(q + 1) * d]
                            last = pe.transpose(ps[n % 4][0:d, tok(q)], a, ident)
                        last.then_inc(hdT_psum.sem, 1)
                phase_end(pe, "pe")

                def unit(u):
                    m, hh, t = units[l][u]
                    q_, k_ = {"mla": (mqT, mkT), "swa": (sqT, skT), "gqa": (gqT, gkT)}[m]
                    kh = hh if m == "mla" else hh // 2
                    nk = 4 if t >= 2 else 2
                    vcol = {"mla": None, "swa": C_SV, "gqa": C_GV}[m]
                    v = [mkv[:, s, hh * P + HD:(hh + 1) * P] if m == "mla" else pj[:, s, vcol + kh * HD:vcol + (kh + 1) * HD]
                         for s in range(nk)]
                    return q_[:, hh, tok(t)], k_[:, kh, 0:nk * P], v, nk

                for s in range(NU[l] + 2):
                    if s < NU[l]:
                        q_, k_, _, nk = unit(s)
                        if s >= 2:
                            pe.wait_ge(probs_ready.sem, probs_ready.at(l, s - 1))
                        mm(ps[s % 2][:, 0:nk * P], q_, k_, start=True, stop=True).then_inc(scores_psum.sem, 1)
                    if 0 <= s - 1 < NU[l]:
                        u = s - 1
                        nk = unit(u)[3]
                        pe.wait_ge(probs_ready.sem, probs_ready.at(l, u + 1))
                        if u >= 2:
                            pe.wait_ge(probT_ready.sem, probT_ready.at(l, u - 1))
                        for j in range(nk):
                            last = pe.transpose(ps[2 + u % 2][:, tok(j)], prob[u % 2][:, tok(j)], ident)
                        last.then_inc(probT_psum.sem, 1)
                    if 0 <= s - 2:
                        u = s - 2
                        _, _, v, nk = unit(u)
                        pe.wait_ge(probT_ready.sem, probT_ready.at(l, u + 1))
                        if u >= 2:
                            pe.wait_ge(head_done.sem, head_done.at(l, u - 1))
                        for j in range(nk):
                            last = mm(ps[4 + u % 2][:, 0:HD], probT[u % 2][:, j, :], v[j], start=(j == 0), stop=(j == nk - 1))
                        last.then_inc(value_psum.sem, 1)
                phase_end(pe, "pe")

                for i, t in enumerate(OUT_TILES[l]):
                    for half in range(2):
                        n = 2 * i + half
                        if n >= 2:
                            pe.wait_ge(mixT_ready.sem, mixT_ready.at(l, n - 1))
                        for k in range(4):
                            last = pe.transpose(ps[n % 2][:, tok(k)], mix[:, t, tok(4 * half + k)], ident)
                        last.then_inc(mixT_psum.sem, 1)
                pe.wait_ge(wout_loaded.sem, wout_loaded.at(l, 1))
                for i, t in enumerate(OUT_TILES[l]):
                    pe.wait_ge(mixT_ready.sem, mixT_ready.at(l, 2 * i + 2))
                    for half in range(2):
                        n = 2 * i + half
                        if n >= 2:
                            pe.wait_ge(resid_ready.sem, resid_ready.at(l, n - 1))
                        for k in range(KD):
                            last = mm(ps[2 + n % 2][:], mixT[:, k, tok(t)], wout[:, k, 512 * half:512 * half + 512],
                                      start=(k == 0), stop=(k == KD - 1))
                        last.then_inc(out_psum.sem, 1)
                phase_end(pe, "pe")
                norm(2 * l + 1, OUT_TILES[l])
                phase_end(pe, "pe")

                pe.wait_ge(router_loaded.sem, router_loaded.at(l, 1))
                for i, t in enumerate(OUT_TILES[l]):
                    for k in range(KD):
                        last = mm(ps[7][:, NE * i:NE * (i + 1)], hT[:, k, tok(t)], rw[:, k, :], start=(k == 0), stop=(k == KD - 1))
                last.then_inc(router_psum.sem, 1)

                def shared_gu(i):
                    t = OUT_TILES[l][i]
                    if i >= 2:
                        pe.wait_ge(sh_act.sem, sh_act.at(l, i - 1))
                    for half in range(2):
                        for k in range(KD):
                            last = mm(ps[2 * (i % 2) + half][:, 0:DE], hT[:, k, tok(t)], sgu[:, k, DE * half:DE * (half + 1)],
                                      start=(k == 0), stop=(k == KD - 1))
                    last.then_inc(sh_gu.sem, 1)

                pe.wait_ge(shared_loaded.sem, shared_loaded.at(l, 2))
                shared_gu(0)
                pe.wait_ge(mask_ready.sem, mask_ready.at(l, 1))
                n_t = NOUT[l]
                for i in range(n_t + 1):
                    for j in range(min(i + 1, n_t)):
                        last = mm(ps[6][:, NE * i:NE * (i + 1)], K("str_b") if j == i else ones, mask[:, j, :],
                                  start=(j == 0), stop=(j == min(i, n_t - 1)))
                last.then_inc(pos_psum.sem, 1)
                for i in range(n_t):
                    if i + 1 < n_t:
                        shared_gu(i + 1)
                    pe.wait_ge(sh_act.sem, sh_act.at(l, i + 1))
                    if i >= 1:
                        pe.wait_ge(sh_aT.sem, sh_aT.at(l, i))
                    for k in range(KE):
                        last = pe.transpose(ps[7][:, tok(k)], act_[:, tok(k)], ident)
                    last.then_inc(sh_aT_psum.sem, 1)
                    pe.wait_ge(sh_aT.sem, sh_aT.at(l, i + 1))
                    if i >= 1:
                        pe.wait_ge(sh_y.sem, sh_y.at(l, 2 * i))
                    for half in range(2):
                        for k in range(KE):
                            last = mm(ps[4 + half][:], actT[:, k, :], sdn[:, k, 512 * half:512 * half + 512],
                                      start=(k == 0), stop=(k == KE - 1))
                    last.then_inc(sh_dn.sem, 1)
                phase_end(pe, "pe")

                def slots_transposed(X, n, m, b):
                    pe.wait_ge(X["gathered"][b].sem, X["gathered"][b].at(l, uses(X, n, m) + 1))
                    pe.wait_ge(X["hT"].sem, X["hT"].at(l, n))
                    for k in range(KD):
                        last = pe.transpose(ps[k // 4][:, tok(k % 4)], hg[b][:, tok(k)], ident)
                    last.then_inc(X["hT_psum"].sem, 1)

                def gate_up(X, n, m, b):
                    pe.wait_ge(X["w"][b % 2].sem, X["w"][b % 2].at(l, RING // 2 * m + (b // 2 + 1)))
                    pe.wait_ge(X["hT"].sem, X["hT"].at(l, n + 1))
                    pe.wait_ge(X["act"].sem, X["act"].at(l, n))
                    for half in range(2):
                        for k in range(KD):
                            last = mm(ps[2 + half][:, 0:DE], hgT[b % 2][:, k, :], wgu[b % 2][:, k, DE * half:DE * (half + 1)],
                                      start=(k == 0), stop=(k == KD - 1))
                    last.then_inc(X["gu"].sem, 1)

                def down(X, n, b):
                    pe.wait_ge(X["act"].sem, X["act"].at(l, n + 1))
                    pe.wait_ge(X["aT"].sem, X["aT"].at(l, n))
                    for k in range(KE):
                        last = pe.transpose(ps[6][:, tok(k)], act_[:, tok(k)], ident)
                    last.then_inc(X["aT_psum"].sem, 1)
                    pe.wait_ge(X["aT"].sem, X["aT"].at(l, n + 1))
                    pe.wait_ge(X["y"].sem, X["y"].at(l, 2 * n))
                    for half in range(2):
                        for k in range(KE):
                            last = mm(ps[4 + half][:], actT[:, k, :], wdn[b % 2][:, k, 512 * half:512 * half + 512],
                                      start=(k == 0), stop=(k == KE - 1))
                    last.then_inc(X["dn"].sem, 1)

                X = EX["first"]
                slots_transposed(X, 0, 0, 0)
                with pe.Fori(0, NE // RING) as i:
                    for b in range(RING):
                        n = RING * i + b
                        gate_up(X, n, i, b)
                        slots_transposed(X, RING * i + (b + 1), i + (b + 1) // RING, (b + 1) % RING)
                        down(X, n, b)
                phase_end(pe, "pe")

                def pe_more(X, l, r, e, n, m, b):
                    slots_transposed(X, n, m, b)
                    gate_up(X, n, m, b)
                    down(X, n, b)

                more_slots(pe, l, pe_more, ["hT_psum", "gu", "aT_psum", "dn"])
                phase_end(pe, "pe")
                phase_end(pe, "pe")

        @block.scalar
        def _(act):
            fn = act.activation
            act.wait_ge(cond_loaded.sem, 32)
            fn(scol, ccol, ACT.Silu).then_inc(cond_silu.sem, 1)
            phase_end(act, "act")

            def norm(u, tiles):
                for i, t in enumerate(tiles):
                    fn(h[:, t, :], xs[:, t, :], ACT.Square, accum_out=stat[:, i:i + 1]).then_inc(squares_ready.sem, 1)
                act.wait_ge(meansq_ready.sem, meansq_ready.at(u, 1))
                fn(stat[:, 8:8 + len(tiles)], stat[:, 4:4 + len(tiles)], ACT.Sqrt).then_inc(std_ready.sem, 1)
                for i, t in enumerate(tiles):
                    for half in range(2):
                        act.wait_ge(hT_psum.sem, hT_psum.at(u, 2 * i + half + 1))
                        fn(hT[:, 4 * half:4 * half + 4, tok(t)], ps[(2 * i + half) % 4][:].rearrange("p (k n) -> p k n", k=4),
                           ACT.Copy).then_inc(hT_ready.sem, 1)

            for l in LAYERS:
                norm(2 * l, ALL)
                phase_end(act, "act")
                act.wait_ge(pads_ready.sem, pads_ready.at(l, 2))
                for ct in range(6):
                    act.wait_ge(qkvT_psum.sem, qkvT_psum.at(l, ct + 1))
                    fn(conv_in[:, ct, :, 2:2 + CTX], ps[ct % 2][:].rearrange("p (s n) -> p s n", s=2), ACT.Copy
                       ).then_inc(qkvT_ready.sem, 1)
                for ct in range(6):
                    act.wait_ge(conv_ready.sem, conv_ready.at(l, ct + 1))
                    fn(conv_out[:, ct, :], conv_out[:, ct, :], ACT.Silu).then_inc(conv_silu.sem, 1)
                for n in range(2 * NT):
                    t, half = divmod(n, 2)
                    act.wait_ge(tok_psum.sem, tok_psum.at(l, n + 1))
                    fn(qkv[:, t, 384 * half:384 * half + 384], ps[n % 2][:, 0:384], ACT.Copy).then_inc(tok_ready.sem, 1)
                phase_end(act, "act")
                act.wait_ge(gate_in.sem, gate_in.at(l, 1))
                fn(ge, ge, ACT.Exp).then_inc(gate_act.sem, 1)
                fn(gn, srow("a_log"), ACT.Exp).then_inc(gate_act.sem, 1)
                act.wait_ge(gate_in.sem, gate_in.at(l, 2))
                fn(ge, ge, ACT.Ln).then_inc(gate_act.sem, 1)
                fn(beta, pj[:, :, C_B:C_B + 8], ACT.Sigmoid).then_inc(gate_act.sem, 1)
                act.wait_ge(qk_meansq.sem, qk_meansq.at(l, 1))
                fn(grs, gsum, ACT.Sqrt).then_inc(qk_std.sem, 1)
                for n in range(2 * NT):
                    t, which = divmod(n, 2)
                    act.wait_ge(qkT_psum.sem, qkT_psum.at(l, n + 1))
                    fn((kT if which else qT)[:, :, tok(t)], ps[n % 2][0:HD, :].rearrange("p (k n) -> p k n", k=HEADS), ACT.Copy
                       ).then_inc(qkT_ready.sem, 1)
                phase_end(act, "act")

                flat = lambda m: m.rearrange("p h j -> p (h j)")
                for b in range(NB):
                    def copy(step, dst, bank, f=ACT.Copy, w=512):
                        act.wait_ge(g_pe.sem, g_pe.after(l, b, step))
                        fn(dst, ps[bank][:, 0:w], f).then_inc(g_act.sem, 1)

                    if b:
                        act.wait_ge(g_dve.sem, g_dve.after(l, b - 1, "out"))
                    copy("sums", ecol, 7, ACT.Exp, 12)
                    copy("decay", flat(M_E), 0, ACT.Exp)
                    copy("decayT", flat(M_ET), 1, ACT.Exp)
                    copy("n2", flat(M_Z), 5)
                    copy("n2T", flat(M_P), 6)
                    copy("n4", flat(M_N), 5)
                    copy("n4T", flat(M_NT), 6)
                    copy("n8", flat(M_Z), 5)
                    for w in ("32", "64", "128"):
                        copy("P" + w, flat(M_P), 5)
                        copy("z" + w, flat(M_Z), 6)
                    copy("vn", vn.rearrange("p h d -> p (h d)"), 1, w=HEADS * HD)
                phase_end(act, "act")

                act.wait_ge(lat_meansq.sem, lat_meansq.at(l, 1))
                fn(asum[:, 0:24], asum[:, 0:24], ACT.Sqrt).then_inc(lat_std.sem, 1)
                fn(zs, pj[:, :, C_Z:C_Z + 256], ACT.Silu).then_inc(lat_std.sem, 1)
                for t in range(NT):
                    act.wait_ge(cT_psum.sem, cT_psum.at(l, t + 1))
                    fn(cT[:, :, tok(t)], ps[t % 2][:, 0:384].rearrange("p (k n) -> p k n", k=3), ACT.Copy
                       ).then_inc(cT_ready.sem, 1)
                for t in range(NT):
                    act.wait_ge(up_psum.sem, up_psum.at(l, 2 * t + 1))
                    fn(mq[:, t, :], ps[2 + t % 2][:, 0:HEADS * MLA_D], ACT.Copy).then_inc(upq_ready.sem, 1)
                phase_end(act, "act")
                act.wait_ge(hd_meansq.sem, hd_meansq.at(l, 1))
                fn(asum[:, 0:100], asum[:, 0:100], ACT.Sqrt).then_inc(hd_std.sem, 1)
                for t in range(NT):
                    for j, (dst, n_h, d) in enumerate(((mqT, 4, MLA_D), (mkT, 4, MLA_D), (sqT, 4, HD), (skT, 2, HD),
                                                       (gqT, 4, HD), (gkT, 2, HD))):
                        n = 6 * t + j
                        act.wait_ge(hdT_psum.sem, hdT_psum.at(l, n + 1))
                        fn(dst[:, :, tok(t)], ps[n % 4][0:d, 0:n_h * P].rearrange("p (k n) -> p k n", k=n_h), ACT.Copy
                           ).then_inc(hdT_ready.sem, 1)
                phase_end(act, "act")

                n_sink = 0
                for s in range(NU[l] + 1):
                    if s < NU[l]:
                        m, hh, t = units[l][s]
                        nk = 4 if t >= 2 else 2
                        row = arow[:, s % 4, :]
                        act.wait_ge(negmax_ready.sem, negmax_ready.at(l, s + 1))
                        if s >= 2:
                            act.wait_ge(probT_psum.sem, probT_psum.at(l, s - 1))
                        if s >= 4:
                            act.wait_ge(head_done.sem, head_done.at(l, s - 3))
                        if m == "swa":
                            fn(row[:, 3:4], srow("sink")[:, hh:hh + 1], ACT.Exp, bias=row[:, 1:2]).then_inc(sink_ready.sem, 1)
                        fn(prob[s % 2][:, 0:nk * P], ps[s % 2][:, 0:nk * P], ACT.Exp, bias=row[:, 1:2],
                           scale=(MLA_D if m == "mla" else HD) ** -0.5, accum_out=row[:, 2:3]).then_inc(probs_ready.sem, 1)
                    if s >= 1:
                        u = s - 1
                        nk = 4 if units[l][u][2] >= 2 else 2
                        act.wait_ge(probT_psum.sem, probT_psum.at(l, u + 1))
                        if u >= 2:
                            act.wait_ge(value_psum.sem, value_psum.at(l, u - 1))
                        fn(probT[u % 2][:, 0:nk, :], ps[2 + u % 2][:, 0:nk * P].rearrange("p (k n) -> p k n", k=nk), ACT.Copy
                           ).then_inc(probT_ready.sem, 1)
                phase_end(act, "act")
                for i, t in enumerate(OUT_TILES[l]):
                    for half in range(2):
                        n = 2 * i + half
                        act.wait_ge(mixT_psum.sem, mixT_psum.at(l, n + 1))
                        fn(mixT[:, 4 * half:4 * half + 4, tok(t)], ps[n % 2][:].rearrange("p (k n) -> p k n", k=4), ACT.Copy
                           ).then_inc(mixT_ready.sem, 1)
                phase_end(act, "act")
                norm(2 * l + 1, OUT_TILES[l])
                phase_end(act, "act")
                act.wait_ge(router_psum.sem, router_psum.at(l, 1))
                fn(scores[:, 0:NOUT[l], :], ps[7][:, 0:NE * NOUT[l]].rearrange("p (t e) -> p t e", e=NE), ACT.Sigmoid
                   ).then_inc(sigmoid_ready.sem, 1)
                for i, t in enumerate(OUT_TILES[l]):
                    act.wait_ge(sh_gu.sem, sh_gu.at(l, i + 1))
                    if i:
                        act.wait_ge(sh_act.sem, sh_act.at(l, i))
                    fn(sgb, ps[2 * (i % 2)][:, 0:DE], ACT.Silu).then_inc(sh_silu.sem, 1)
                    act.wait_ge(sh_aT_psum.sem, sh_aT_psum.at(l, i + 1))
                    fn(actT, ps[7][:, 0:DE].rearrange("p (k n) -> p k n", k=KE), ACT.Copy).then_inc(sh_aT.sem, 1)
                    act.wait_ge(sh_dn.sem, sh_dn.at(l, i + 1))
                    fn(acc[:, t, 0:512], ps[4][:], ACT.Copy).then_inc(sh_y.sem, 1)
                phase_end(act, "act")

                def act_expert(X, l, r, e, n, m, b):
                    act.wait_ge(X["gu"].sem, X["gu"].at(l, n + 1))
                    act.wait_ge(X["act"].sem, X["act"].at(l, n))
                    fn(sgb, ps[2][:, 0:DE], ACT.Silu).then_inc(X["silu"].sem, 1)
                    act.wait_ge(X["aT_psum"].sem, X["aT_psum"].at(l, n + 1))
                    act.wait_ge(X["dn"].sem, X["dn"].at(l, n))
                    fn(actT, ps[6][:, 0:DE].rearrange("p (k n) -> p k n", k=KE), ACT.Copy).then_inc(X["aT"].sem, 1)
                    act.wait_ge(X["dn"].sem, X["dn"].at(l, n + 1))
                    act.wait_ge(X["scattered"][b].sem, X["scattered"][b].at(l, uses(X, n, m)))
                    fn(yo[b][:, 0:512], ps[4][:], ACT.Copy).then_inc(X["y"].sem, 1)

                with act.Fori(0, NE // RING) as i:
                    for b in range(RING):
                        act_expert(EX["first"], l, 0, None, RING * i + b, i, b)
                phase_end(act, "act")
                more_slots(act, l, act_expert, ["silu", "aT", "y"])
                phase_end(act, "act")
                phase_end(act, "act")

        @block.vector
        def _(dve):
            count = [0]

            def link(ins):
                count[0] += 1
                ins.then_inc(dve_step, 1)
                dve.wait_ge(dve_step, count[0])

            tt, ts, stt, red = dve.tensor_tensor, dve.tensor_scalar, dve.scalar_tensor_tensor, dve.tensor_reduce
            for l in LAYERS:
                dve.wait_ge(modb_loaded.sem, modb_loaded.at(l, 6))
                for j in range(12):
                    n = 12 * l + j
                    dve.wait_ge(modp_psum.sem, n + 1)
                    if j == 0 and l:
                        dve.wait_ge(modrow_stored.sem, modrow_stored.at(l - 1, 1))
                    tt(modrow[:, 512 * j:512 * j + 512], ps[n % 2][0:2, :], brow[:, 512 * j:512 * j + 512], ALU.add
                       ).then_inc(modrow_part.sem, 1)
                dve.wait_ge(modrow_part.sem, 12 * (l + 1))
                link(stt(modrow[:, D:2 * D], modrow[:, D:2 * D], 1.0, gains[:, 0, :], ALU.add, ALU.mult))
                stt(modrow[:, 4 * D:5 * D], modrow[:, 4 * D:5 * D], 1.0, gains[:, 1, :], ALU.add, ALU.mult
                    ).then_inc(modrow_ready.sem, 1)
            phase_end(dve, "dve")

            def norm(u, tiles):
                n = len(tiles)
                dve.wait_ge(squares_ready.sem, squares_ready.at(u, n))
                ts(stat[:, 4:4 + n], stat[:, 0:n], 1.0 / D, EPS, ALU.mult, ALU.add).then_inc(meansq_ready.sem, 1)
                dve.wait_ge(std_ready.sem, std_ready.at(u, 1))
                link(dve.reciprocal(stat[:, 12:12 + n], stat[:, 8:8 + n]))
                dve.wait_ge(mod_loaded.sem, mod_loaded.at(u, 6))
                for i, t in enumerate(tiles):
                    s = t // 2
                    link(stt(h[:, t, :], xs[:, t, :], stat[:, 12 + i:13 + i], mod[:, 1, s, :], ALU.mult, ALU.mult))
                    tt(h[:, t, :], h[:, t, :], mod[:, 0, s, :], ALU.add).then_inc(h_ready.sem, 1)

            def group_meansq(dst, src, sq, d, eps=EPS, scale=None):
                link(tt(sq, src, src, ALU.mult))
                link(red(dst, sq, AX, ALU.add))
                return ts(dst, dst, 1.0 / d if scale is None else scale, eps, ALU.mult, ALU.add)

            for l in LAYERS:
                norm(2 * l, ALL)
                phase_end(dve, "dve")
                dve.wait_ge(small_loaded.sem, small_loaded.at(l, N_SMALL + 6))
                dve.wait_ge(pads_ready.sem, pads_ready.at(l, 2))
                for ct in range(6):
                    dve.wait_ge(qkvT_ready.sem, qkvT_ready.at(l, ct + 1))
                    o = conv_out[:, ct, :].rearrange("p (s n) -> p s n", s=2)
                    link(ts(o, conv_in[:, ct, :, 0:CTX], convw[:, ct, 0:1], None, ALU.mult))
                    for j in range(1, CONV):
                        ins = stt(o, conv_in[:, ct, :, j:j + CTX], convw[:, ct, j:j + 1], o, ALU.mult, ALU.add)
                        if j < CONV - 1:
                            link(ins)
                        else:
                            ins.then_inc(conv_ready.sem, 1)
                for n in range(NCHUNK * NT):
                    ch, t = divmod(n, NT)
                    dve.wait_ge(proj_psum.sem, proj_psum.at(l, n + 1))
                    dve.tensor_copy(pj[:, t, ch * CW:(ch + 1) * CW], ps[2 + n % 4][:, 0:CW]).then_inc(proj_ready.sem, 1)
                phase_end(dve, "dve")

                link(tt(gz, pj[:, :, C_A:C_A + 8], bc(srow("dt_bias"), 1, NT), ALU.add))
                link(ts(ge, gz, -1.0, None, ALU.mult))
                tt(ge, ge, gz, ALU.min).then_inc(gate_in.sem, 1)
                dve.wait_ge(gate_act.sem, gate_act.at(l, 2))
                ts(ge, ge, 1.0, None, ALU.add).then_inc(gate_in.sem, 1)
                dve.wait_ge(gate_act.sem, gate_act.at(l, 3))
                link(stt(gz, gz, 0.0, ge, ALU.max, ALU.add))
                link(stt(la, gz, -1.0, bc(gn, 1, NT), ALU.mult, ALU.mult))
                qk = qkv[:, :, 0:512]
                link(tt(gsq, qk, qk, ALU.mult))
                link(red(gsum, heads4(gsq), AX, ALU.add))
                ts(gsum, gsum, EPS, None, ALU.add).then_inc(qk_meansq.sem, 1)
                dve.wait_ge(qk_std.sem, qk_std.at(l, 1))
                link(dve.reciprocal(grs, grs))
                link(ts(grs[:, :, 0:HEADS], grs[:, :, 0:HEADS], HD ** -0.5, None, ALU.mult))
                tt(heads4(qk), heads4(qk), bc(grs, 3, HD), ALU.mult).then_inc(qk_normed.sem, 1)
                phase_end(dve, "dve")

                dve.memset(S, 0.0).then_inc(state_zero.sem, 1)
                for b in range(NB):
                    d, t = divmod(b, NT)
                    if d:
                        t = (1, 0, 3, 2)[t]
                    if d and b == NT:
                        dve.wait_ge(g_dve.sem, g_dve.after(l, b - 1, "out"))
                        dve.memset(S, 0.0).then_inc(state_zero.sem, 1)
                    inc, strict = K("inc_b" if d else "inc_f"), K("str_b" if d else "str_f")
                    hs = slice(HEADS * d, HEADS * d + HEADS)
                    over_h = lambda m: bc(m, 1, HEADS)

                    def done(ins):
                        ins.then_inc(g_dve.sem, 1)

                    bank = lambda i: ps[i][:].rearrange("p (h j) -> p h j", h=HEADS)
                    half = lambda i, at=0: ps[i][:, at:at + HEADS * HD].rearrange("p (h j) -> p h j", h=HEADS)
                    link(tt(M_X, over_h(strict), bc(la[:, t, hs], 2, P), ALU.mult))
                    done(tt(M_Y, over_h(inc), bc(la[:, t, hs], 2, P), ALU.mult))
                    dve.wait_ge(g_act.sem, g_act.after(l, b, "decay"))
                    dve.wait_ge(g_pe.sem, g_pe.after(l, b, "kk"))
                    link(tt(M_L, bank(2), M_E, ALU.mult))
                    link(tt(M_L, M_L, over_h(strict), ALU.mult))
                    done(tt(M_L, M_L, bc(beta[:, t, hs], 2, P), ALU.mult))
                    dve.wait_ge(g_dve.sem, g_dve.after(l, b, "a"))
                    done(stt(M_N, M_L, -1.0, over_h(K("b16")), ALU.mult, ALU.mult))
                    link(tt(M_B32, M_L, over_h(K("m32")), ALU.mult))
                    link(tt(M_B64, M_L, over_h(K("m64")), ALU.mult))
                    done(tt(M_B128, M_L, over_h(K("m128")), ALU.mult))
                    dve.wait_ge(g_act.sem, g_act.after(l, b, "decayT"))
                    dve.wait_ge(g_pe.sem, g_pe.after(l, b, "kq"))
                    link(tt(M_QK, bank(3), M_ET, ALU.mult))
                    done(tt(M_QK, M_QK, over_h(inc), ALU.mult))
                    dve.wait_ge(g_pe.sem, g_pe.after(l, b, "aT"))
                    link(stt(M_NT, bank(4), -1.0, over_h(K("b16")), ALU.mult, ALU.mult))
                    done(tt(M_PT, M_NT, over_h(ident), ALU.add))
                    for step, was in (("p1", "pt0"), ("p2", "pt1"), ("p3", "pt2")):
                        dve.wait_ge(g_dve.sem, g_dve.after(l, b, was))
                        dve.wait_ge(g_pe.sem, g_pe.after(l, b, step))
                        done(tt(M_PT, M_PT, bank(4), ALU.add))
                    for w, was in (("32", "pt3"), ("64", "pt32"), ("128", "pt64")):
                        dve.wait_ge(g_dve.sem, g_dve.after(l, b, was))
                        dve.wait_ge(g_pe.sem, g_pe.after(l, b, "pz" + w))
                        done(tt(M_PT, M_PT, bank(4), ALU.subtract))
                    dve.wait_ge(g_pe.sem, g_pe.after(l, b, "ks"))
                    link(tt(vx, half(0), bc(ecol[:, 0:4], 2, HD), ALU.mult))
                    link(tt(vx, heads4(qkv[:, t, 512:768]), vx, ALU.subtract))
                    done(tt(vx, vx, bc(beta[:, t, hs], 2, HD), ALU.mult))
                    dve.wait_ge(g_act.sem, g_act.after(l, b, "vn"))
                    done(tt(vns, vn, bc(ecol[:, 4:8], 2, HD), ALU.mult))
                    dve.wait_ge(g_pe.sem, g_pe.after(l, b, "o"))
                    o = heads4(og[:, t, :])
                    link(tt(vx, half(0, HEADS * HD), bc(ecol[:, 0:4], 2, HD), ALU.mult))
                    if d:
                        link(tt(vx, vx, o, ALU.add))
                    link(tt(o, vx, half(2), ALU.add))
                    dve.wait_ge(g_pe.sem, g_pe.after(l, b, "s"))
                    link(tt(S, S, bc(ecol[0:HD, 8:12], 2, HD), ALU.mult))
                    done(tt(S, S, ps[3][0:HD, 0:HEADS * HD].rearrange("p (h j) -> p h j", h=HEADS), ALU.add))
                phase_end(dve, "dve")

                cq, ckv, kr = pj[:, :, C_MQ:C_MQ + 256], pj[:, :, C_MKV:C_MKV + 128], pj[:, :, C_MKR:C_MKR + 32]
                s16 = lambda a: asum[:, a:a + 16].rearrange("p (t g) -> p t g", t=NT)
                link(group_meansq(s16(0), heads4(og), heads4(osq), HD))
                link(group_meansq(asum[:, 16:20], cq, osq, MLA_QR))
                group_meansq(asum[:, 20:24], ckv, osq[:, :, 0:128], MLA_KVR).then_inc(lat_meansq.sem, 1)
                dve.wait_ge(lat_std.sem, lat_std.at(l, 2))
                link(dve.reciprocal(asum[:, 0:24], asum[:, 0:24]))
                link(tt(cq, cq, bc(asum[:, 16:20], 2, MLA_QR), ALU.mult))
                link(tt(ckv, ckv, bc(asum[:, 20:24], 2, MLA_KVR), ALU.mult))
                link(tt(cq, cq, bc(srow("qn"), 1, NT), ALU.mult))
                tt(ckv, ckv, bc(srow("kvn"), 1, NT), ALU.mult).then_inc(lat_ready.sem, 1)
                m0 = heads4(mix[:, :, 0:256])
                link(tt(heads4(og), heads4(og), bc(s16(0), 3, HD), ALU.mult))
                link(tt(heads4(og), heads4(og), bc(bc(srow("gdn_g"), 1, HEADS), 1, NT), ALU.mult))
                tt(m0, heads4(og), heads4(zs), ALU.mult)
                for t in range(NT):
                    dve.wait_ge(up_psum.sem, up_psum.at(l, 2 * t + 2))
                    dve.tensor_copy(mkv[:, t, :], ps[4 + t % 2][:]).then_inc(upkv_ready.sem, 1)
                phase_end(dve, "dve")

                mq_h = mq.rearrange("p t (h d) -> p (t h) d", h=HEADS)
                mkv_h = mkv.rearrange("p t (h d) -> p (t h) d", h=HEADS)
                mkf_h = mkf.rearrange("p t (h d) -> p (t h) d", h=HEADS)
                sqk, gqk = heads4(pj[:, :, C_SQ:C_SQ + 384]), heads4(pj[:, :, C_GQ:C_GQ + 384])
                q_no, q_pe, k_no = mq_h[:, :, 0:64], mq_h[:, :, 64:96], mkv_h[:, :, 0:64]
                wide = carve(arena, 13040, 16, HD)
                narrow = carve(arena, 13040, 16, MLA_ROPE)
                six = carve(arena, 13040, NT, 6, HD)
                s24 = lambda a: asum[:, a:a + 24].rearrange("p (t g) -> p t g", t=NT)
                link(group_meansq(asum[:, 0:16], q_no, wide, MLA_NOPE))
                link(group_meansq(asum[:, 16:32], q_pe, narrow, MLA_ROPE))
                link(group_meansq(asum[:, 32:48], k_no, wide, MLA_NOPE))
                link(group_meansq(asum[:, 48:52], kr, carve(arena, 13040, NT, MLA_ROPE), MLA_ROPE))
                link(group_meansq(s24(52), sqk, six, HD))
                group_meansq(s24(76), gqk, six, HD).then_inc(hd_meansq.sem, 1)
                dve.wait_ge(hd_std.sem, hd_std.at(l, 1))
                link(dve.reciprocal(asum[:, 0:100], asum[:, 0:100]))
                g = srow("mla_qk")
                link(tt(q_no, q_no, bc(asum[:, 0:16], 2, 64), ALU.mult))
                link(tt(q_pe, q_pe, bc(asum[:, 16:32], 2, 32), ALU.mult))
                link(tt(mkf_h[:, :, 0:64], k_no, bc(asum[:, 32:48], 2, 64), ALU.mult))
                link(tt(kr, kr, bc(asum[:, 48:52], 2, 32), ALU.mult))
                link(tt(sqk, sqk, bc(s24(52), 3, HD), ALU.mult))
                link(tt(gqk, gqk, bc(s24(76), 3, HD), ALU.mult))
                link(tt(mq_h, mq_h, bc(g[:, 0:96], 1, 16), ALU.mult))
                link(tt(mkf_h[:, :, 0:64], mkf_h[:, :, 0:64], bc(g[:, 96:160], 1, 16), ALU.mult))
                link(tt(kr, kr, bc(g[:, 160:192], 1, NT), ALU.mult))
                for v, r in ((sqk, srow("swa_qk")), (gqk, srow("gqa_qk"))):
                    link(tt(v[:, :, 0:4, :], v[:, :, 0:4, :], bc(bc(r[:, 0:HD], 1, 4), 1, NT), ALU.mult))
                    link(tt(v[:, :, 4:6, :], v[:, :, 4:6, :], bc(bc(r[:, HD:2 * HD], 1, 2), 1, NT), ALU.mult))

                def rope(v, cos, sin, n1, n2, d2):
                    a = carve(arena, 13040, n1, n2 * 2 * d2)
                    b = carve(arena, 13040 + 1024, n1, n2 * 2 * d2)
                    link(tt(a, v, cos, ALU.mult))
                    pair = lambda w: w.rearrange("p a (b q r) -> p a b q r", q=2, r=d2)
                    for q in range(2):
                        link(tt(pair(b)[:, :, :, q, :], pair(v)[:, :, :, 1 - q, :], pair(sin)[:, :, :, q, :], ALU.mult))
                    return tt(v, a, b, ALU.add)

                cos_hd, sin_hd = K("cos_hd", 2, 384), K("sin_hd", 2, 384)
                pe8 = lambda n: K(n, 8, MLA_ROPE)
                pe2 = lambda n: K(n, 2, HEADS * MLA_ROPE)[:, :, 0:MLA_ROPE]
                link(rope(pj[:, 2:4, C_SQ:C_SQ + 384], cos_hd, sin_hd, 2, 12, 16))
                link(rope(pj[:, 2:4, C_GQ:C_GQ + 384], cos_hd, sin_hd, 2, 12, 16))
                link(rope(mq_h[:, 8:16, 64:96], pe8("cos_pe"), pe8("sin_pe"), 8, 2, 8))
                link(rope(kr[:, 2:4, :], pe2("cos_pe"), pe2("sin_pe"), 2, 2, 8))
                dve.tensor_copy(mkf.rearrange("p t (h d) -> p t h d", h=HEADS)[:, :, :, 64:96], bc(kr, 2, HEADS)
                                ).then_inc(heads_ready.sem, 1)
                phase_end(dve, "dve")

                n_sink = 0
                for s in range(NU[l] + 2):
                    if s < NU[l]:
                        m, hh, t = units[l][s]
                        nk = 4 if t >= 2 else 2
                        row = arow[:, s % 4, :]
                        dve.wait_ge(scores_psum.sem, scores_psum.at(l, s + 1))
                        scale = (MLA_D if m == "mla" else HD) ** -0.5
                        if m == "swa" and t >= 2:
                            far = K("window", 2, SEQ)[:, t - 2, :]
                            link(tt(ps[s % 2][:, CTX:], ps[s % 2][:, CTX:], far, ALU.add))
                        link(red(row[:, 0:1], ps[s % 2][:, 0:nk * P], AX, ALU.max))
                        if m == "swa":
                            link(stt(row[:, 0:1], row[:, 0:1], scale, srow("sink")[:, hh:hh + 1], ALU.mult, ALU.max))
                            scale = 1.0
                        ts(row[:, 1:2], row[:, 0:1], -scale, None, ALU.mult).then_inc(negmax_ready.sem, 1)
                    if s >= 2:
                        u = s - 2
                        m, hh, t = units[l][u]
                        row = arow[:, u % 4, :]
                        dve.wait_ge(value_psum.sem, value_psum.at(l, u + 1))
                        total = row[:, 2:3]
                        if m == "swa":
                            n_sink += 1
                            dve.wait_ge(sink_ready.sem, sink_ready.at(l, n_sink))
                            link(tt(row[:, 4:5], row[:, 2:3], row[:, 3:4], ALU.add))
                            total = row[:, 4:5]
                        link(dve.reciprocal(row[:, 5:6], total))
                        col = {"mla": 256, "swa": 512, "gqa": 768}[m] + hh * HD
                        ts(mix[:, t, col:col + HD], ps[4 + u % 2][:, 0:HD], row[:, 5:6], None, ALU.mult
                           ).then_inc(head_done.sem, 1)
                phase_end(dve, "dve")

                for i, t in enumerate(OUT_TILES[l]):
                    for half in range(2):
                        n = 2 * i + half
                        cols = slice(512 * half, 512 * half + 512)
                        dve.wait_ge(out_psum.sem, out_psum.at(l, n + 1))
                        link(tt(tmp_o, ps[2 + n % 2][:], mod[:, 2, t // 2, cols], ALU.mult))
                        tt(xs[:, t, cols], xs[:, t, cols], tmp_o, ALU.add).then_inc(resid_ready.sem, 1)
                        dve.wait_ge(resid_ready.sem, resid_ready.at(l, n + 1))
                phase_end(dve, "dve")
                norm(2 * l + 1, OUT_TILES[l])
                phase_end(dve, "dve")

                n_t = NOUT[l]
                dve.wait_ge(sigmoid_ready.sem, sigmoid_ready.at(l, 1))
                link(tt(sel[:, 0:n_t, :], scores[:, 0:n_t, :], bc(srow("rbias"), 1, n_t), ALU.add))
                for i in range(n_t):
                    link(dve.max(out=top8[:, i, :], in_=sel[:, i, :]))
                    link(dve.max_index(out=idx8[:, i, :], in_max=top8[:, i, :], in_values=sel[:, i, :]))
                link(dve.tensor_copy(idxf[:, 0:n_t, :], idx8[:, 0:n_t, :]))
                for i in range(n_t):
                    link(tt(onehot[i], bc(K("experts"), 1, TOPK), bc(idxf[:, i, 0:TOPK], 2, NE), ALU.is_equal))
                    link(red(mask[:, i, :], onehot[i].rearrange("p k e -> p e k"), AX, ALU.add))
                    link(tt(ohp, onehot[i], bc(scores[:, i, :], 1, TOPK), ALU.mult))
                    link(red(gate[:, i, 0:TOPK], ohp, AX, ALU.add))
                dve.nop().then_inc(mask_ready.sem, 1)
                link(red(gatesum[:, 0:n_t], gate[:, 0:n_t, 0:TOPK], AX, ALU.add))
                link(dve.reciprocal(gatesum[:, 0:n_t], gatesum[:, 0:n_t]))
                link(stt(gate[:, 0:n_t, 0:TOPK], gate[:, 0:n_t, 0:TOPK], ROUTED, bc(gatesum[:, 0:n_t], 2, TOPK),
                         ALU.mult, ALU.mult))
                dve.wait_ge(pos_psum.sem, pos_psum.at(l, 1))
                link(dve.tensor_copy(pos[:, 0:n_t, :], ps[6][:, 0:n_t * NE].rearrange("p (t e) -> p t e", e=NE)))
                link(red(cntmax[:, 0:1], ps[6][:, n_t * NE:(n_t + 1) * NE], AX, ALU.max))
                link(dve.tensor_copy(maxcnt[0:1, 0:1], cntmax[0:1, 0:1]))
                for i in range(n_t):
                    link(tt(ohp, onehot[i], bc(pos[:, i, :], 1, TOPK), ALU.mult))
                    link(red(posk[:, i, 0:TOPK], ohp, AX, ALU.add))
                stt(addr[:, 0:n_t, 0:TOPK], posk[:, 0:n_t, 0:TOPK], float(NE), idxf[:, 0:n_t, 0:TOPK], ALU.mult, ALU.add
                    ).then_inc(addr_ready.sem, 1)
                for i, t in enumerate(OUT_TILES[l]):
                    dve.wait_ge(sh_silu.sem, sh_silu.at(l, i + 1))
                    if i:
                        dve.wait_ge(sh_aT_psum.sem, sh_aT_psum.at(l, i))
                    tt(act_, sgb, ps[2 * (i % 2) + 1][:, 0:DE], ALU.mult).then_inc(sh_act.sem, 1)
                    dve.wait_ge(sh_dn.sem, sh_dn.at(l, i + 1))
                    dve.tensor_copy(acc[:, t, 512:1024], ps[5][:]).then_inc(sh_y.sem, 1)
                dve.wait_ge(lists_loaded.sem, lists_loaded.at(l, 1))
                dve.wait_ge(tail_ready.sem, tail_ready.at(l, 1))
                ts(lsg[:, 0:R[l], :], lst[:, 0:R[l], :], 3, None, ALU.logical_shift_right)
                phase_end(dve, "dve")

                def slots_copied(X, n, b):
                    dve.wait_ge(X["hT_psum"].sem, X["hT_psum"].at(l, n + 1))
                    dve.tensor_copy(hgT[b % 2][:, 0:4, :], ps[0][:].rearrange("p (k n) -> p k n", k=4))
                    dve.tensor_copy(hgT[b % 2][:, 4:8, :], ps[1][:].rearrange("p (k n) -> p k n", k=4)).then_inc(X["hT"].sem, 1)

                def times_up(X, n):
                    dve.wait_ge(X["silu"].sem, X["silu"].at(l, n + 1))
                    dve.wait_ge(X["aT_psum"].sem, X["aT_psum"].at(l, n))
                    tt(act_, sgb, ps[3][:, 0:DE], ALU.mult).then_inc(X["act"].sem, 1)

                def y_copied(X, n, m, b):
                    dve.wait_ge(X["dn"].sem, X["dn"].at(l, n + 1))
                    dve.wait_ge(X["scattered"][b].sem, X["scattered"][b].at(l, uses(X, n, m)))
                    dve.tensor_copy(yo[b][:, 512:1024], ps[5][:]).then_inc(X["y"].sem, 1)

                X = EX["first"]
                slots_copied(X, 0, 0)
                with dve.Fori(0, NE // RING) as i:
                    for b in range(RING):
                        times_up(X, RING * i + b)
                        slots_copied(X, RING * i + (b + 1), b + 1)
                        y_copied(X, RING * i + b, i, b)
                phase_end(dve, "dve")

                def dve_more(X, l, r, e, n, m, b):
                    slots_copied(X, n, b)
                    times_up(X, n)
                    y_copied(X, n, m, b)

                more_slots(dve, l, dve_more, ["hT", "act", "y"])
                phase_end(dve, "dve")
                for i, t in enumerate(OUT_TILES[l]):
                    dve.wait_ge(yrow_loaded[i % 2].sem, yrow_loaded[i % 2].at(l, i // 2 + 1))
                    for k in range(TOPK):
                        ins = stt(acc[:, t, :], yrow[i % 2][:, k, :], gate[:, i, k:k + 1], acc[:, t, :], ALU.mult, ALU.add)
                        if k < TOPK - 1:
                            link(ins)
                        else:
                            ins.then_inc(y_added.sem, 1)
                    dve.wait_ge(y_added.sem, y_added.at(l, i + 1))
                    link(tt(acc[:, t, :], acc[:, t, :], mod[:, 2, t // 2, :], ALU.mult))
                    link(tt(xs[:, t, :], xs[:, t, :], acc[:, t, :], ALU.add))
                phase_end(dve, "dve")

        @block.gpsimd
        def _(pool):
            by_dma = [s for kind in EX for s in EX[kind]["gathered"] + EX[kind]["scattered"]]
            for s in started:
                if s not in by_dma:
                    pool.sem_inc(s.sem, s.start)
            rows_bound = pool.to_reg(NT * P - 1)
            codes_bound = pool.to_reg(NT * P * CODES - 1)
            phase_end(pool, "pool")
            for l in LAYERS:
                phase_end(pool, "pool")
                pool.memset(conv_in[:, :, :, 0:2], 0.0).then_inc(pads_ready.sem, 1)
                pool.memset(conv_in[:, :, :, CTX + 2:CTX + 4], 0.0).then_inc(pads_ready.sem, 1)
                for _ in range(7):
                    phase_end(pool, "pool")
                phase_end(pool, "pool")
                n_t = NOUT[l]
                pool.memset(nocode, NO_CODE).then_inc(nocode_ready.sem, 1)
                pool.memset(lst[:, 0:R[l], NE:NL], NO_CODE).then_inc(tail_ready.sem, 1)
                pool.iota(code[:, 0:n_t, :], pattern=[[P * CODES, n_t], [1, CODES]], base=0, channel_multiplier=CODES
                          ).then_inc(code_ready.sem, 1)
                pool.wait_ge(code_ready.sem, code_ready.at(l, 1))
                pool.wait_ge(lists_cleared.sem, lists_cleared.at(l, 1))
                pool.wait_ge(addr_ready.sem, addr_ready.at(l, 1))
                for i in range(n_t):
                    for k in range(TOPK):
                        pool.indirect_dma_start(out=list_d, out_offset=bass.IndirectOffsetOnAxis(ap=addr[:, i, k:k + 1], axis=0),
                                                in_=code[:, i, k:k + 1], in_offset=None).then_inc(listed.sem, 16)
                phase_end(pool, "pool")

                def waited():
                    pool.sem_inc(pool_go, 1)

                def rows_in(b, signal):
                    pool.indirect_dma_start(out=hg[b], out_offset=None, in_=h_d,
                                            in_offset=bass.IndirectOffsetOnAxis(ap=gidx[:, b, :], axis=0),
                                            bounds_check=rows_bound, oob_is_err=False).then_inc(signal.sem, 16)

                def rows_out(b, signal):
                    pool.indirect_dma_start(out=y_d, out_offset=bass.IndirectOffsetOnAxis(ap=sidx[:, b, :], axis=0),
                                            in_=yo[b], in_offset=None, bounds_check=codes_bound, oob_is_err=False
                                            ).then_inc(signal.sem, 16)

                def gather(X, r, e, n, m, b, free):
                    pool.wait_ge(X["hT_psum"].sem, X["hT_psum"].at(l, free))
                    pool.wait_ge(X["gathered"][b].sem, X["gathered"][b].at(l, uses(X, n, m)))
                    waited()
                    pool.tensor_copy(gidx[:, b, :], lsg[:, r, bass.ds(e, 1)]).then_inc(X["g_idx"].sem, 1)
                    pool.wait_ge(X["g_idx"].sem, X["g_idx"].at(l, n + 1))
                    waited()
                    rows_in(b, X["gathered"][b])

                def scatter(X, r, e, n, m, b):
                    pool.wait_ge(X["scattered"][b].sem, X["scattered"][b].at(l, uses(X, n, m)))
                    waited()
                    pool.tensor_copy(sidx[:, b, :], lst[:, r, bass.ds(e, 1)]).then_inc(X["s_idx"].sem, 1)
                    pool.wait_ge(X["s_idx"].sem, X["s_idx"].at(l, n + 1))
                    pool.wait_ge(X["y"].sem, X["y"].at(l, 2 * n + 2))
                    waited()
                    rows_out(b, X["scattered"][b])

                X = EX["first"]
                for b in range(RING):
                    pool.memset(hg[b], 0.0).then_inc(pool_step, 1)
                    pool.memset(yo[b], 0.0).then_inc(pool_step, 1)
                pool.memset(gidx[:], NO_CODE).then_inc(pool_step, 1)
                pool.memset(sidx[:], NO_CODE).then_inc(pool_step, 1)
                pool.wait_ge(pool_step, (2 * RING + 2) * (l + 1))
                if l == 0:
                    for Y in EX.values():
                        for b in range(1 if Y["serial"] else RING):
                            rows_in(b, Y["gathered"][b])
                            pool.wait_ge(Y["gathered"][b].sem, 16)
                            rows_out(b, Y["scattered"][b])
                            pool.wait_ge(Y["scattered"][b].sem, 16)
                for n in range(AHEAD):
                    gather(X, 0, n, n, 0, n, 0)
                with pool.Fori(0, NE // RING) as i:
                    for b in range(RING):
                        e = RING * i + (b + AHEAD)
                        gather(X, 0, e, e, i + (b + AHEAD) // RING, (b + AHEAD) % RING, RING * i + b)
                        scatter(X, 0, RING * i + b, RING * i + b, i, b)
                for b in range(RING):
                    pool.wait_ge(X["scattered"][b].sem, X["scattered"][b].at(l, NE // RING))
                phase_end(pool, "pool")

                def pool_more(X, l, r, e, n, m, b):
                    gather(X, r, e, n, m, b, n)
                    scatter(X, r, e, n, m, b)

                more_slots(pool, l, pool_more, ["g_idx", "s_idx"])
                phase_end(pool, "pool")
                phase_end(pool, "pool")


_INS = ["x", "c", "ctx", "c_ctx", "w_mod", "b_mod", "norm1_g", "norm2_g", "w_in", "gdn_conv_w", "gdn_a_log",
        "gdn_dt_bias", "gdn_norm_g", "mla_qn_g", "mla_kvn_g", "mla_w_uq", "mla_w_ukv", "mla_qk_g", "swa_qk_g", "swa_sink",
        "gqa_qk_g", "w_out", "router_w", "router_bias", "exp_w_gu", "exp_w_down", "shared_w_gu", "shared_w_down"]


def kernel(**inputs):
    import concourse.bacc as bacc
    from concourse.bass_utils import run_bass_kernel_spmd

    nc = bacc.Bacc("TRN2", target_bir_lowering=False, num_devices=1)
    arrays, args = {}, []
    for name in _INS:
        a = np.ascontiguousarray(inputs[name])
        arrays[f"in_{name}"] = a
        args.append(nc.dram_tensor(f"in_{name}", a.shape, mybir.dt.from_np(a.dtype), kind="ExternalInput").ap())
    arrays["consts"] = constants()
    args.append(nc.dram_tensor("consts", [P, N_CONST], F32, kind="ExternalInput").ap())
    args.append(nc.dram_tensor("out_0", [1, SEQ, D], F32, kind="ExternalOutput").ap())
    build(nc, *args)
    r = run_bass_kernel_spmd(nc, [arrays], core_ids=[0])
    return r.results[0]["out_0"]
```
